# Optimizing a Trainium2 kernel written in Bass

```python
import math
import jax, jax.numpy as jnp
from jax import lax
import numpy as np

D_MODEL = 1024
BATCH = 1
SEQ = 512
DEPTH = 2

N_MIXERS = 2
N_CONV_LAYERS = (DEPTH + 1) // 2
N_SSM_LAYERS = DEPTH // 2
CONV_WIDTH = 3
SSM_GROUP = 16
SSM_GROUPS = D_MODEL // SSM_GROUP
SSM_STATE = 64
SSM_CHUNK = 128
DT_MIN = 1e-3
DT_MAX = 1e-1
EIG_CLIP = -1e-4
D_FF = 2816
MEM_LEN = 256
XA_HEADS = 4
XA_HEAD_DIM = D_MODEL // XA_HEADS
NORM_EPS = 1e-6
N_NORMS = 5

kernel_name = "hybrid_conv_s5_macaron_decoder"

def rmsnorm(x, g):
    xf = x.astype(jnp.float32)
    y = xf * lax.rsqrt(jnp.mean(xf * xf, axis=-1, keepdims=True) + NORM_EPS)
    return (y * g.astype(jnp.float32)).astype(x.dtype)

def swiglu_ffn(h, w_up, w_down):
    gate, up = jnp.split(h @ w_up, 2, axis=-1)
    return (jax.nn.silu(gate) * up) @ w_down

def short_conv_mixer(h, w_in, conv_w, w_out):
    c_gate, b_gate, v = jnp.split(h @ w_in, 3, axis=-1)
    u = c_gate * v
    conv = lax.conv_general_dilated(
        u, conv_w[:, None, :],
        window_strides=(1,),
        padding=[(CONV_WIDTH - 1, 0)],
        dimension_numbers=("NWC", "WIO", "NWC"),
        feature_group_count=D_MODEL)
    return (b_gate * conv) @ w_out

def _complex_scan_op(e1, e2):
    a1r, a1i, b1r, b1i = e1
    a2r, a2i, b2r, b2i = e2
    return (a2r * a1r - a2i * a1i,
            a2r * a1i + a2i * a1r,
            a2r * b1r - a2i * b1i + b2r,
            a2r * b1i + a2i * b1r + b2i)

def s5_mixer(h, a_re, a_im, log_dt, b_re, b_im, c_re, c_im, d_skip, w_glu):
    bsz, seq, _ = h.shape
    f32 = jnp.float32
    lam_re = jnp.minimum(a_re.astype(f32), EIG_CLIP)
    lam_im = a_im.astype(f32)
    dt = jnp.exp(log_dt.astype(f32))[:, None]
    mag = jnp.exp(lam_re * dt)
    abar_re = mag * jnp.cos(lam_im * dt)
    abar_im = mag * jnp.sin(lam_im * dt)
    den = lam_re * lam_re + lam_im * lam_im
    num_re = abar_re - 1.0
    num_im = abar_im
    coef_re = (num_re * lam_re + num_im * lam_im) / den
    coef_im = (num_im * lam_re - num_re * lam_im) / den
    br = b_re.astype(f32)
    bi = b_im.astype(f32)
    bbar_re = coef_re[..., None] * br - coef_im[..., None] * bi
    bbar_im = coef_re[..., None] * bi + coef_im[..., None] * br
    cr = c_re.astype(f32)
    ci = c_im.astype(f32)

    n_chunks = seq // SSM_CHUNK
    u = h.astype(f32).reshape(bsz, n_chunks, SSM_CHUNK, SSM_GROUPS, SSM_GROUP)
    u = jnp.moveaxis(u, 1, 0)
    el_shape = (bsz, SSM_CHUNK, SSM_GROUPS, SSM_STATE)
    a_el_re = jnp.broadcast_to(abar_re, el_shape)
    a_el_im = jnp.broadcast_to(abar_im, el_shape)

    def chunk_step(carry, u_c):
        h_re, h_im = carry
        bu_re = jnp.einsum("btgh,gph->btgp", u_c, bbar_re)
        bu_im = jnp.einsum("btgh,gph->btgp", u_c, bbar_im)
        acc_re, acc_im, loc_re, loc_im = lax.associative_scan(
            _complex_scan_op, (a_el_re, a_el_im, bu_re, bu_im), axis=1)
        s_re = loc_re + acc_re * h_re[:, None] - acc_im * h_im[:, None]
        s_im = loc_im + acc_re * h_im[:, None] + acc_im * h_re[:, None]
        y_c = (jnp.einsum("btgp,ghp->btgh", s_re, cr)
               - jnp.einsum("btgp,ghp->btgh", s_im, ci))
        return (s_re[:, -1], s_im[:, -1]), y_c

    h0 = (jnp.zeros((bsz, SSM_GROUPS, SSM_STATE), f32),
          jnp.zeros((bsz, SSM_GROUPS, SSM_STATE), f32))
    _, y = lax.scan(chunk_step, h0, u)
    y = jnp.moveaxis(y, 0, 1).reshape(bsz, seq, D_MODEL)
    y = y + d_skip.astype(f32) * h.astype(f32)
    z = jax.nn.gelu(y).astype(h.dtype)
    val, gate = jnp.split(z @ w_glu, 2, axis=-1)
    return val * jax.nn.sigmoid(gate)

def memory_cross_attention(h, mem_n, w_q, w_kv, w_o):
    bsz, seq, _ = h.shape
    mlen = mem_n.shape[1]
    q = (h @ w_q).reshape(bsz, seq, XA_HEADS, XA_HEAD_DIM)
    k, v = jnp.split(mem_n @ w_kv, 2, axis=-1)
    k = k.reshape(bsz, mlen, XA_HEADS, XA_HEAD_DIM)
    v = v.reshape(bsz, mlen, XA_HEADS, XA_HEAD_DIM)
    s = jnp.einsum("bqhd,bkhd->bhqk", q, k).astype(jnp.float32) * (XA_HEAD_DIM ** -0.5)
    p = jax.nn.softmax(s, axis=-1).astype(v.dtype)
    o = jnp.einsum("bhqk,bkhd->bqhd", p, v).reshape(bsz, seq, D_MODEL)
    return o @ w_o

def setup_inputs(seed: int = 0) -> dict:
    key = jax.random.key(seed)
    ks = jax.random.split(key, 24)
    D = D_MODEL
    nrm = jax.random.normal

    def w(k, shape, fan_in):
        return nrm(k, shape, jnp.float32) * (fan_in ** -0.5)

    x = nrm(ks[0], (BATCH, SEQ, D), jnp.float32)
    mem = nrm(ks[1], (BATCH, MEM_LEN, D), jnp.float32)
    norm_g = 1.0 + 0.02 * nrm(ks[2], (DEPTH, N_NORMS, D), jnp.float32)
    final_g = 1.0 + 0.02 * nrm(ks[3], (D,), jnp.float32)
    ffn1_up = w(ks[4], (DEPTH, D, 2 * D_FF), D)
    ffn1_down = w(ks[5], (DEPTH, D_FF, D), D_FF)
    ffn2_up = w(ks[6], (DEPTH, D, 2 * D_FF), D)
    ffn2_down = w(ks[7], (DEPTH, D_FF, D), D_FF)
    conv_w_in = w(ks[8], (N_CONV_LAYERS, D, 3 * D), D)
    conv_w = w(ks[9], (N_CONV_LAYERS, CONV_WIDTH, D), CONV_WIDTH)
    conv_w_out = w(ks[10], (N_CONV_LAYERS, D, D), D)
    ssm_shape = (N_SSM_LAYERS, SSM_GROUPS, SSM_STATE)
    ssm_a_re = -0.5 + 0.01 * nrm(ks[11], ssm_shape, jnp.float32)
    ssm_a_im = (math.pi * jnp.arange(SSM_STATE, dtype=jnp.float32)[None, None, :]
                + 0.01 * nrm(ks[12], ssm_shape, jnp.float32))
    ssm_log_dt = jax.random.uniform(ks[13], (N_SSM_LAYERS, SSM_GROUPS), jnp.float32,
                                    math.log(DT_MIN), math.log(DT_MAX))
    ssm_b_re = w(ks[14], (N_SSM_LAYERS, SSM_GROUPS, SSM_STATE, SSM_GROUP), 2 * SSM_GROUP)
    ssm_b_im = w(ks[15], (N_SSM_LAYERS, SSM_GROUPS, SSM_STATE, SSM_GROUP), 2 * SSM_GROUP)
    ssm_c_re = w(ks[16], (N_SSM_LAYERS, SSM_GROUPS, SSM_GROUP, SSM_STATE), SSM_STATE)
    ssm_c_im = w(ks[17], (N_SSM_LAYERS, SSM_GROUPS, SSM_GROUP, SSM_STATE), SSM_STATE)
    ssm_d = nrm(ks[18], (N_SSM_LAYERS, D), jnp.float32)
    ssm_w_glu = w(ks[19], (N_SSM_LAYERS, D, 2 * D), D)
    xa_w_q = w(ks[20], (DEPTH, D, D), D)
    xa_w_kv = w(ks[21], (DEPTH, D, 2 * D), D)
    xa_w_o = w(ks[22], (DEPTH, D, D), D)
    return {"x": x, "mem": mem, "norm_g": norm_g, "final_g": final_g,
            "ffn1_up": ffn1_up, "ffn1_down": ffn1_down,
            "ffn2_up": ffn2_up, "ffn2_down": ffn2_down,
            "conv_w_in": conv_w_in, "conv_w": conv_w, "conv_w_out": conv_w_out,
            "ssm_a_re": ssm_a_re, "ssm_a_im": ssm_a_im, "ssm_log_dt": ssm_log_dt,
            "ssm_b_re": ssm_b_re, "ssm_b_im": ssm_b_im,
            "ssm_c_re": ssm_c_re, "ssm_c_im": ssm_c_im,
            "ssm_d": ssm_d, "ssm_w_glu": ssm_w_glu,
            "xa_w_q": xa_w_q, "xa_w_kv": xa_w_kv, "xa_w_o": xa_w_o}

def reference(x, mem, norm_g, final_g, ffn1_up, ffn1_down, ffn2_up, ffn2_down,
              conv_w_in, conv_w, conv_w_out,
              ssm_a_re, ssm_a_im, ssm_log_dt, ssm_b_re, ssm_b_im,
              ssm_c_re, ssm_c_im, ssm_d, ssm_w_glu,
              xa_w_q, xa_w_kv, xa_w_o):
    for i in range(DEPTH):
        g = norm_g[i]
        x = x + 0.5 * swiglu_ffn(rmsnorm(x, g[0]), ffn1_up[i], ffn1_down[i])
        h = rmsnorm(x, g[1])
        j = i // N_MIXERS
        if i % N_MIXERS == 0:
            x = x + short_conv_mixer(h, conv_w_in[j], conv_w[j], conv_w_out[j])
        else:
            x = x + s5_mixer(h, ssm_a_re[j], ssm_a_im[j], ssm_log_dt[j],
                             ssm_b_re[j], ssm_b_im[j], ssm_c_re[j], ssm_c_im[j],
                             ssm_d[j], ssm_w_glu[j])
        x = x + memory_cross_attention(rmsnorm(x, g[2]), rmsnorm(mem, g[3]),
                                       xa_w_q[i], xa_w_kv[i], xa_w_o[i])
        x = x + 0.5 * swiglu_ffn(rmsnorm(x, g[4]), ffn2_up[i], ffn2_down[i])
    return rmsnorm(x, final_g)


_drawn_inputs = setup_inputs


def setup_inputs(seed=0):
    import zlib

    import numpy as np

    out = dict(_drawn_inputs(seed))
    spreads = {}
    factors = {'final_g': 26.974,
     'ssm_a_re': 200.0,
     'ssm_a_im': 92.712,
     'ssm_log_dt': 96.224,
     'ssm_b_re': 180.288,
     'ssm_b_im': 180.392,
     'ssm_c_re': 178.952,
     'ssm_c_im': 182.44}
    for name, (base, spread) in spreads.items():
        noise = np.random.default_rng([zlib.crc32(name.encode()), seed]).standard_normal(out[name].shape)
        drawn = base * np.exp(spread * noise) if base else spread * noise
        out[name] = __import__('jax').numpy.asarray(drawn.astype(out[name].dtype))
    for name, factor in factors.items():
        out[name] = (out[name] * factor).astype(out[name].dtype)
    return out
```

```python
import math
from contextlib import ExitStack

import concourse.bass as bass
from concourse import mybir

ALU = mybir.AluOpType
ACT = mybir.ActivationFunctionType
AX = mybir.AxisListType
F32 = mybir.dt.float32
F32R = mybir.dt.float32r
I32 = mybir.dt.int32

P = 128
D = 1024
KD = D // P
SEQ = 512
MEM = 256
FF = 2816
KF = FF // P
DEPTH = 2
HEADS = 4
HD = D // HEADS
SLOTS = 4
LEAD = 3
UT = 8
EPS = 1e-6
DT_T = 4
NCH = SEQ // DT_T
QT = 8
NT = 32
G_FINAL = DEPTH * 5 * KD
G_CONV = G_FINAL + KD
G_SKIP = G_CONV + 3 * KD
NCOLS = G_SKIP + KD


def cut(x, bits, parts):
    out = []
    for _ in range(parts):
        m, e = math.frexp(x)
        out.append(math.ldexp(round(math.ldexp(m, bits)), e - bits))
        x -= out[-1]
    return out


TWO_PI = cut(2 * math.pi, 9, 4)
MAGIC = 12582912.0


CUTS = [(0, 8), (8, 16), (16, KF)]


def plan():
    phases, u, t, c = [], 0, 0, 0
    sizes = {"conv_cv": (2 * KD, 2 * KD, 0), "conv_b": (KD, KD, KD), "conv_o": (KD, KD, 0), "s5": (0, 0, KD),
             "glu": (2 * KD, 2 * KD, 0), "k": (KD, KD, 0), "v": (8, 4, 0), "q": (KD, KD, KD), "core": (0, 0, 0), "o": (KD, KD, 0)}
    for layer in range(DEPTH):
        mixer = ["conv_cv", "conv_b", "conv_o"] if layer % 2 == 0 else ["s5", "glu"]
        for kind in ["ffn1"] + mixer + ["k", "v", "q", "core", "o", "ffn2"]:
            if kind[:3] != "ffn":
                todo = [(kind, None, sizes[kind])]
            elif (kind, layer) in (("ffn2", 0), ("ffn1", 1)):
                todo = []
                for f0, f1 in CUTS:
                    n = f1 - f0
                    todo += [("up", (f0, f1), (2 * n, 2 * n, n)), ("down", (f0, f1), (KD, KD, 0))]
            else:
                todo = [("up", (0, KF), (2 * KF, 2 * KF, KF)), ("down", (0, KF), (3 * KD, KD, 0))]
            for name, part, (du, dt, dc) in todo:
                phases.append((name, layer, u, t, c, part))
                u, t, c = u + du, t + dt, c + dc
    return phases, u


def build(nc, x_in, mem_in, cols_in, w8, wd, s5p, s5bc, scratch, out):
    phases, UNITS = plan()
    RESID = [i for i, ph in enumerate(phases) if ph[0] in ("conv_o", "glu", "o") or ph[0] == "down" and ph[5][1] == KF]

    def norm_of(i):
        return 1 + max([n for n, r in enumerate(RESID) if r < i], default=-1)

    def gain_col(n):
        if n == len(RESID):
            return G_FINAL
        nxt = phases[RESID[n - 1] + 1] if n else phases[0]
        which = {"conv_cv": 1, "s5": 1, "k": 2, "up": 0 if n % 4 == 0 else 4}[nxt[0]]
        return (nxt[1] * 5 + which) * KD

    deferred = [n for n in range(len(RESID) + 1) if n < len(RESID) and not (n and phases[RESID[n - 1] + 1][0] == "s5")]
    h_base = {n: KD * k for k, n in enumerate(deferred)}

    with ExitStack() as ctx:
        def sem(name):
            return ctx.enter_context(nc.semaphore(name))

        top = [(nc.sbuf_base + 31) // 32 * 32]

        def at(name, shape, dt, offset):
            return nc.alloc_sbuf_tensor_at(name, shape, dt, offset=offset)

        def size(shape):
            n = 4
            for s in shape[1:]:
                n *= s
            return (n + 31) // 32 * 32

        def sb(name, shape, dt=F32):
            t = at(name, shape, dt, top[0])
            top[0] += size(shape)
            assert top[0] <= nc.sbuf_usable_end, (name, top[0])
            return t

        X = sb("X", [P, KD, SEQ])
        h_at = top[0]
        h_hi = sb("h_hi", [P, KD, SEQ], F32R)
        h_lo = sb("h_lo", [P, KD, SEQ], F32R)
        raw = sb("raw", [P, SLOTS, UT * P])
        w_hi = sb("w_hi", [P, SLOTS, UT * P], F32R)
        w_lo = sb("w_lo", [P, SLOTS, UT * P], F32R)
        g_buf = sb("g_buf", [P, 2, SEQ])
        t_buf = sb("t_buf", [P, 2, SEQ])
        u_buf = sb("u_buf", [P, SEQ])
        a_buf = sb("a_buf", [P, 2, SEQ])
        rstd = sb("rstd", [P, SEQ])
        nt_a = sb("nt_a", [P, SEQ])
        small = sb("small", [P, 3, SEQ // P])
        sq_at = top[0]
        sq = sb("sq", [P, SEQ])
        ssq = sb("ssq", [P, SEQ])
        ident = sb("ident", [P, P])
        ones = sb("ones", [P, P])
        cols = sb("cols", [P, NCOLS])
        mx = sb("mx", [P, 2, 4])
        nb = sb("nb", [P, 2, 4])
        esum = sb("esum", [P, 2, 4])
        rsum = sb("rsum", [P, 2, 4])

        area = top[0]

        class Area:
            def __init__(self, start):
                self.at = start

            def take(self, name, shape, dt=F32):
                t = at(name, shape, dt, self.at)
                self.at += size(shape)
                assert self.at <= nc.sbuf_usable_end, (name, self.at)
                return t

        ffn = Area(area)
        f_hi = ffn.take("f_hi", [P, KF, SEQ], F32R)
        f_lo = ffn.take("f_lo", [P, KF, SEQ], F32R)
        mid = Area(area)
        m_hi = mid.take("m_hi", [P, KD, SEQ], F32R)
        m_lo = mid.take("m_lo", [P, KD, SEQ], F32R)
        conv = Area(mid.at)
        cu = conv.take("cu", [P, KD, SEQ + 2])
        cv = conv.take("cv", [P, KD, SEQ])
        att = Area(mid.at)
        k_hi = att.take("k_hi", [P, KD, MEM], F32R)
        k_lo = att.take("k_lo", [P, KD, MEM], F32R)
        v_hi = att.take("v_hi", [P, 2, D], F32R)
        v_lo = att.take("v_lo", [P, 2, D], F32R)
        mem_at = max(att.at, conv.at)
        ma = Area(mem_at)
        n_hi = ma.take("n_hi", [P, KD, MEM], F32R)
        n_lo = ma.take("n_lo", [P, KD, MEM], F32R)
        mT = ma.take("mT", [P, KD, MEM])
        mb = Area(mem_at)
        pt_hi = mb.take("pt_hi", [P, 2, SEQ], F32R)
        pt_lo = mb.take("pt_lo", [P, 2, SEQ], F32R)
        prob = mb.take("prob", [P, 2, 4, MEM])
        STAGE = 26 * QT * 32
        s5 = Area(mid.at)
        mag4 = s5.take("mag4", [P, NT])
        prep = Area(s5.at + 4 * STAGE)
        stage = [s5.take(f"stage{i}", [P, STAGE]) for i in range(2)]

        def cut_stage(t):
            e, f = 8 * QT * 32, 18 * QT * 32
            return (t[:, 0:e].rearrange("p (r i k s) -> p r k i s", r=2, i=QT, k=4), t[:, e:f].rearrange("p (r k i s) -> p r k i s", r=2, k=5, i=QT),
                    t[:, f:].rearrange("p (r i n) -> p r i n", r=2, i=QT))
        pin = prep.take("pin", [P, 3, NT])
        tmp = prep.take("tmp", [P, 12, NT])
        tmpi = prep.take("tmpi", [P, NT], I32)
        pw = prep.take("pw", [P, 2, 5, NT])
        un = prep.take("un", [P, 2, 7, NT])
        coef = prep.take("coef", [P, 2, NT])
        bcq = prep.take("bcq", [P, 4, QT * 32])
        w0 = prep.take("w0", [P, 4 * QT * 32])
        w1 = prep.take("w1", [P, 4 * QT * 32])
        u4 = at("u4", [P, QT, NCH], F32, sq_at)
        s5h = Area(h_at)
        uq = s5h.take("uq", [P, 2, 2, DT_T, NCH])
        ET = s5h.take("ET", [P, 2, QT, P])
        r0 = s5h.take("r0", [P, QT, NCH])
        r1 = s5h.take("r1", [P, QT, NCH])
        r2 = s5h.take("r2", [P, QT, NCH])
        r3 = s5h.take("r3", [P, QT, NCH])
        assert s5h.at <= h_at + 2 * size([P, KD, SEQ])
        MB = s5.take("MB", [P, 2, 4, P])

        PS = ctx.enter_context(nc.psum_tensor("PS", [P, 8, 512], F32))
        NORM_BANK = 4

        raw_in = [sem(f"raw_in{i}") for i in range(SLOTS)]
        w_hi_done = sem("w_hi_done")
        w_lo_done = sem("w_lo_done")
        unit_done = sem("unit_done")
        tile_done = sem("tile_done")
        x_in_done = [sem(f"x_in_done{i}") for i in range(4)]
        cols_done = sem("cols_done")
        mem_done = sem("mem_done")
        s5p_done = sem("s5p_done")
        bc_done = sem("bc_done")
        spilled = sem("spilled")
        stage_in = [sem(f"stage_in{i}") for i in range(2)]
        out_done = sem("out_done")
        const_done = sem("const_done")
        ident0 = sem("ident0")
        h_hi_done = sem("h_hi_done")
        h_lo_done = sem("h_lo_done")
        sq_done = sem("sq_done")
        ssq_done = sem("ssq_done")
        sum_done = sem("sum_done")
        newton = sem("newton")
        diag_done = sem("diag_done")
        spread_done = sem("spread_done")
        g_done = sem("g_done")
        tanh_done = sem("tanh_done")
        u_done = sem("u_done")
        c_ready = sem("c_ready")
        c_hi_done = sem("c_hi_done")
        c_lo_done = sem("c_lo_done")
        kv_hi_done = sem("kv_hi_done")
        n_hi_done = sem("n_hi_done")
        n_lo_done = sem("n_lo_done")
        conv_step = sem("conv_step")
        score_done = sem("score_done")
        bias_done = sem("bias_done")
        att_step = sem("att_step")
        exp_done = sem("exp_done")
        prob_done = sem("prob_done")
        pt_done = sem("pt_done")
        pt_hi_done = sem("pt_hi_done")
        pt_lo_done = sem("pt_lo_done")
        pv_done = sem("pv_done")
        o_hi_done = sem("o_hi_done")
        o_lo_done = sem("o_lo_done")
        prep_step = sem("prep_step")
        den_done = sem("den_done")
        rden_done = sem("rden_done")
        s5_step = sem("s5_step")
        s5_tr = sem("s5_tr")
        s5_et = sem("s5_et")
        s5_mb0 = sem("s5_mb0")
        s5_u = sem("s5_u")
        s5_u4a = sem("s5_u4a")
        s5_u4v = sem("s5_u4v")
        s5_x = sem("s5_x")
        s5_xfree = sem("s5_xfree")
        s5_s = sem("s5_s")
        s5_y = sem("s5_y")
        y_done = sem("y_done")
        y2_done = sem("y2_done")
        y_arg = sem("y_arg")
        y_tanh = sem("y_tanh")
        fin = sem("fin")

        ssq_order = []
        for i, (kind, layer, *_rest) in enumerate(phases):
            if i == 0:
                ssq_order.append(("x", 0))
            if kind in ("conv_cv", "glu"):
                ssq_order.append(("mem", layer))
            if i in RESID:
                ssq_order.append(("x", RESID.index(i) + 1))

        def ssq_index(kind, n):
            return ssq_order.index((kind, n))

        block = ctx.enter_context(nc.Block())

        def groups(eng, n, body, peel_first=False, peel_last=False):
            a, b = int(peel_first), n - int(peel_last)
            if peel_first:
                body(0)
            if b - a == 1:
                body(a)
            elif b > a:
                with eng.Fori(a, b) as g:
                    body(g)
            if peel_last and n > 1:
                body(n - 1)

        last_phase = len(phases) - 1

        @block.sync
        def _(sp):
            w8_at = 0

            def load_x():
                for i in range(4):
                    sp.dma_start(X[:, 2 * i:2 * i + 2, :], x_in[:, 2 * i:2 * i + 2, :]).then_inc(x_in_done[i], 16)

            for kind, layer, u0, t0, c0, part in phases:
                if kind in ("s5", "core"):
                    continue
                d0 = sum(1 for ph in phases if ph[0] == "down" and ph[2] < u0 and ph[5][1] == KF) * KD
                if kind == "down" and part == (0, KF):
                    def body(g):
                        for j in range(4):
                            for c, (a, b) in enumerate(CUTS):
                                i = 3 * j + c
                                sp.wait_ge(w_lo_done, u0 + 12 * g + i - SLOTS + 1)
                                sp.dma_start(raw[:, i % SLOTS, 0:(b - a) * P], wd[d0 + 4 * g + j, :, a * P:b * P])\
                                  .then_inc(raw_in[i % SLOTS], 16)
                    groups(sp, 2, body)
                elif kind == "down":
                    a, b = part

                    def body(g):
                        for i in range(4):
                            sp.wait_ge(w_lo_done, u0 + 4 * g + i - SLOTS + 1)
                            sp.dma_start(raw[:, i, 0:(b - a) * P], wd[d0 + 4 * g + i, :, a * P:b * P]).then_inc(raw_in[i], 16)
                    groups(sp, 2, body)
                else:
                    n = 2 * (part[1] - part[0]) if kind == "up" else {"conv_cv": 16, "glu": 16}.get(kind, 8)

                    def body(g):
                        for i in range(4):
                            if not (isinstance(g, int) and u0 + 4 * g + i < SLOTS):
                                sp.wait_ge(w_lo_done, u0 + 4 * g + i - SLOTS + 1)
                            sp.dma_start(raw[:, i, :], w8[w8_at + 4 * g + i]).then_inc(raw_in[i], 16)
                            if isinstance(g, int) and u0 + 4 * g + i == 0:
                                load_x()
                    groups(sp, n // 4, body, peel_first=(u0 == 0))
                    w8_at += n
            for k in range(KD):
                sp.wait_ge(fin, k + 1)
                sp.dma_start(out[:, k, :], X[:, k, :]).then_inc(out_done, 16)
            sp.wait_ge(out_done, 16 * KD)

        @block.gpsimd
        def _(pool):
            pool.dma_start(cols[:, :], cols_in).then_inc(cols_done, 16)
            pool.memset(ident[:, :], 0.0).then_inc(ident0, 1)
            pool.memset(ones[:, :], 1.0).then_inc(const_done, 1)
            pool.wait_ge(ident0, 1)
            pool.affine_select(out=ident[:, :], in_=ident[:, :], compare_op=ALU.not_equal, fill=1.0,
                               base=0, pattern=[[-1, P]], channel_multiplier=1).then_inc(const_done, 1)
            steps = [0]

            def squares(src, k0, k1, width, ready):
                def one(k):
                    ready(k)
                    pool.tensor_tensor(sq[:, 0:width], src(k), src(k), ALU.mult).then_inc(sq_done, 1)
                    pool.wait_ge(sq_done, steps[0] + 2 * k)
                    return pool.tensor_tensor(ssq[:, 0:width], ssq[:, 0:width], sq[:, 0:width], ALU.add)
                ready(0)
                pool.tensor_tensor(ssq[:, 0:width], src(0), src(0), ALU.mult).then_inc(sq_done, 1)
                pool.wait_ge(sq_done, steps[0] + 1)
                with pool.Fori(1, KD - 1) as k:
                    one(k).then_inc(sq_done, 1)
                    pool.wait_ge(sq_done, steps[0] + 2 * k + 1)
                one(KD - 1).then_inc(ssq_done, 1)
                steps[0] += 2 * KD - 2

            def free_ssq(kind, n):
                if ssq_index(kind, n):
                    pool.wait_ge(sum_done, ssq_index(kind, n))

            M, A, S = ALU.mult, ALU.add, ALU.subtract
            count = [0]

            def step(ins):
                ins.then_inc(prep_step, 1)
                count[0] += 1
                pool.wait_ge(prep_step, count[0])

            def tt(o, a, b, op):
                step(pool.tensor_tensor(o, a, b, op))

            def ts(o, a, s1, s2, op0, op1=ALU.bypass):
                step(pool.tensor_scalar(o, a, s1, s2, op0, op1))

            def parameters():
                T = [tmp[:, j, :] for j in range(12)]
                pool.dma_start(pin[:, :, :], s5p).then_inc(s5p_done, 16)
                pool.dma_start(bcq[:, :, :], s5bc[0]).then_inc(bc_done, 16)
                pool.wait_ge(s5p_done, 16)
                are, aim, ldt = (pin[:, j, :] for j in range(3))
                lre, dt, th, mag, k, r, sn, cs, a, b, c, d = T

                def stt(o, a_, s_, b_, op0, op1):
                    ts(d, a_, s_, None, op0)
                    tt(o, d, b_, op1)

                def exp(o, x):
                    ts(x, x, 88.0, -87.0, ALU.min, ALU.max)
                    ts(k, x, 1.4426950408889634, MAGIC, M, A)
                    ts(k, k, -MAGIC, None, A)
                    stt(r, k, -0.693359375, x, M, A)
                    stt(r, k, 2.12194440e-4, r, M, A)
                    ts(o, r, 1.0 / 5040, None, M)
                    for f in (720, 120, 24, 6, 2, 1):
                        stt(o, o, 1.0 / f, r, A, M)
                    ts(o, o, 1.0, None, A)
                    ts(tmpi[:, :], k, 127.0, 8388608.0, A, M)
                    tt(o, o, tmpi[:, :].bitcast(F32), M)

                ts(lre, are, -1e-4, None, ALU.min)
                ts(a, ldt, 1.0, None, M)
                exp(dt, a)
                tt(th, aim, dt, M)
                tt(a, lre, dt, M)
                exp(mag, a)
                ts(k, th, 0.15915494309189535, MAGIC, M, A)
                ts(k, k, -MAGIC, None, A)
                for piece in TWO_PI:
                    stt(th, k, -piece, th, M, A)
                ts(r, th, 0.5, None, M)
                tt(a, r, r, M)
                sc = [(-1) ** j / math.factorial(2 * j + 1) for j in range(8)]
                cc = [(-1) ** j / math.factorial(2 * j) for j in range(9)]
                ts(sn, a, sc[7], None, M)
                for j in range(6, 0, -1):
                    stt(sn, sn, sc[j], a, A, M)
                stt(sn, sn, 1.0, r, A, M)
                ts(cs, a, cc[8], None, M)
                for j in range(7, 0, -1):
                    stt(cs, cs, cc[j], a, A, M)
                ts(cs, cs, 1.0, None, A)
                tt(b, sn, sn, M)
                stt(c, sn, 2.0, cs, M, M)
                ts(b, b, -2.0, 1.0, M, A)

                def cmul(o, x, y):
                    tt(k, x[0], y[0], M)
                    tt(r, x[1], y[1], M)
                    tt(o[0], k, r, S)
                    tt(k, x[0], y[1], M)
                    tt(r, x[1], y[0], M)
                    tt(o[1], k, r, A)

                pwr = [(pw[:, 0, j, :], pw[:, 1, j, :]) for j in range(5)]
                unr = [(un[:, 0, j, :], un[:, 1, j, :]) for j in range(7)]
                step(pool.memset(pwr[0][0], 1.0))
                step(pool.memset(pwr[0][1], 0.0))
                tt(pwr[1][0], mag, b, M)
                tt(pwr[1][1], mag, c, M)
                cmul(pwr[2], pwr[1], pwr[1])
                cmul(pwr[3], pwr[2], pwr[1])
                cmul(pwr[4], pwr[2], pwr[2])
                cmul((sn, cs), (b, c), (b, c))
                cmul(unr[0], (sn, cs), (sn, cs))
                for v in range(1, 7):
                    cmul(unr[v], unr[v - 1], unr[v - 1])
                tt(mag4[:, :], mag, mag, M)
                tt(mag4[:, :], mag4[:, :], mag4[:, :], M)
                tt(a, lre, lre, M)
                tt(b, aim, aim, M)
                pool.tensor_tensor(a, a, b, A).then_inc(den_done, 1)
                pool.wait_ge(rden_done, 1)
                ts(c, pwr[1][0], -1.0, None, A)
                tt(k, c, lre, M)
                tt(r, pwr[1][1], aim, M)
                tt(k, k, r, A)
                tt(coef[:, 0, :], k, b, M)
                tt(k, pwr[1][1], lre, M)
                tt(r, c, aim, M)
                tt(k, k, r, S)
                tt(coef[:, 1, :], k, b, M)

            def quarters(q0, q1):
                E, F, rot = cut_stage(stage[0])
                for q in range(q0, q1):
                    def op(o, a, b, f):
                        step(pool.tensor_tensor(o, a, b, f))

                    def cplx(o, x, y, t0, t1, neg_im=False):
                        op(t0, x[0], y[0], M)
                        op(t1, x[1], y[1], M)
                        op(o[0], t0, t1, S)
                        op(t0, x[0], y[1], M)
                        op(t1, x[1], y[0], M)
                        if neg_im:
                            step(pool.tensor_scalar(t0, t0, -1.0, None, M))
                        op(o[1], t0, t1, S if neg_im else A)

                    def tiles(ap):
                        return ap.rearrange("p (i f) -> p i f", i=QT)

                    def powers(dst, src, lo, hi, neg):
                        m = hi - lo
                        t = [w[:, 0:m * QT * 32].rearrange("p (k i f) -> p k i f", k=m, i=QT) for w in (w0, w1)]
                        p = [pw[:, j, lo:hi, QT * q:QT * (q + 1)][:, :, :, None].to_broadcast([P, m, QT, 32]) for j in range(2)]
                        cplx([dst[:, j, lo:hi, :, :] for j in range(2)], p,
                             [x[:, None, :, :].to_broadcast([P, m, QT, 32]) for x in src], *t, neg)

                    pool.wait_ge(bc_done, 16 * q + 16)
                    e0 = [E[:, j, 0, :, :] for j in range(2)]
                    cf = [coef[:, j, QT * q:QT * (q + 1)][:, :, None].to_broadcast([P, QT, 32]) for j in range(2)]
                    cplx(e0, cf, (tiles(bcq[:, 0, :]), tiles(bcq[:, 1, :])), tiles(w0[:, 0:QT * 32]), tiles(w1[:, 0:QT * 32]))
                    powers(E, e0, 1, 4, False)
                    step(pool.tensor_copy(F[:, 0, 0, :, :], tiles(bcq[:, 2, :])))
                    step(pool.tensor_scalar(F[:, 1, 0, :, :], tiles(bcq[:, 3, :]), -1.0, None, M))
                    powers(F, (tiles(bcq[:, 2, :]), tiles(bcq[:, 3, :])), 1, 5, True)
                    if q < 3:
                        pool.dma_start(bcq[:, :, :], s5bc[q + 1]).then_inc(bc_done, 16)
                    step(pool.memset(rot[:, 0, :, 0:1], 1.0))
                    step(pool.memset(rot[:, 1, :, 0:1], 0.0))
                    for v in range(7):
                        w = 1 << v
                        t = [x[:, 0:QT * w].rearrange("p (i n) -> p i n", i=QT) for x in (w0, w1)]
                        cplx([rot[:, j, :, w:2 * w] for j in range(2)],
                             [un[:, j, v, QT * q:QT * (q + 1)][:, :, None].to_broadcast([P, QT, w]) for j in range(2)],
                             [rot[:, j, :, 0:w] for j in range(2)], *t)
                    pool.dma_start(scratch[q], stage[0][:, :]).then_inc(spilled, 16)
                    pool.wait_ge(spilled, 16 * q + 16)

            def load_stage(q):
                pool.dma_start(stage[q % 2][:, :], scratch[q]).then_inc(stage_in[q % 2], 16)

            for landed in x_in_done:
                pool.wait_ge(landed, 16)
            squares(lambda k: X[:, k, :], 0, KD, SEQ, lambda k: None)
            for i, (kind, layer, u0, t0, c0, part) in enumerate(phases):
                if kind == "up" and part == CUTS[0]:
                    if layer == 0:
                        pool.wait_ge(unit_done, u0)
                        parameters()
                        quarters(0, 2)
                    else:
                        quarters(2, 4)
                        load_stage(0)
                        load_stage(1)
                if kind == "s5":
                    for q in range(2, 4):
                        pool.wait_ge(s5_y, 2 * (q - 1))
                        load_stage(q)
                if kind == "conv_cv":
                    pool.wait_ge(unit_done, u0)
                    pool.dma_start(mT[:, :, :], mem_in).then_inc(mem_done, 16)
                    free_ssq("mem", layer)
                    pool.wait_ge(mem_done, 16 * (layer + 1))
                    squares(lambda k: mT[:, k, :], 0, KD, MEM, lambda k: None)
                if kind == "glu":
                    pool.wait_ge(c_lo_done, c0)
                    pool.dma_start(mT[:, :, :], mem_in).then_inc(mem_done, 16)
                    free_ssq("mem", layer)
                    pool.wait_ge(mem_done, 16 * (layer + 1))
                    squares(lambda k: mT[:, k, :], 0, KD, MEM, lambda k: None)
                if i in RESID:
                    n = RESID.index(i) + 1
                    free_ssq("x", n)
                    if kind == "glu":
                        squares(lambda k: X[:, k, :], 0, KD, SEQ, lambda k: pool.wait_ge(tile_done, t0 + 2 * k + 2))
                    else:
                        squares(lambda k: X[:, k, :], 0, KD, SEQ, lambda k: pool.wait_ge(tile_done, t0 + k + 1))

        def by_step(ap):
            return ap.rearrange("p (n j) -> p j n", j=DT_T)

        def s5_bank(b):
            return (7, NORM_BANK)[b % 2]

        def s5_u4(copy, r, powers):
            for k in powers:
                for q in range(4):
                    ins = copy(u4[32 * k:32 * k + 32, q:QT:4, :], uq[32 * q:32 * q + 32, r % 2, :, DT_T - 1 - k, :])
            return ins

        def s5_matrices(act, r):
            for b in range(4):
                act.wait_ge(s5_tr, 5 * r + b + 1)
                act.activation(ET[:, b // 2, 4 * (b % 2):4 * (b % 2) + 4, :], PS[:, s5_bank(b), :].rearrange("p (i s) -> p i s", i=4),
                               ACT.Copy).then_inc(s5_et, 1)
            act.wait_ge(s5_tr, 5 * r + 5)
            act.wait_ge(s5_mb0, 1)
            for ch in range(2):
                for q in range(4):
                    s = slice(32 * q, 32 * q + 32)
                    ins = act.activation(MB[s, ch, :, 32 * q:32 * q + 32],
                                         PS[s, s5_bank(4), ch * P:(ch + 1) * P].rearrange("p (l f) -> p l f", l=4), ACT.Copy)
            ins.then_inc(s5_et, 1)

        @block.scalar
        def _(act):
            def split(u, slot):
                if not isinstance(u, int) or u >= SLOTS:
                    act.wait_ge(unit_done, u - SLOTS + 1)
                    act.wait_ge(raw_in[slot], 4 * (u - slot) + 16)
                else:
                    act.wait_ge(raw_in[slot], 16)
                act.activation(w_hi[:, slot, :], raw[:, slot, :], ACT.Copy).then_inc(w_hi_done, 1)

            def ahead(u, i):
                if isinstance(u, int) and u + LEAD >= UNITS:
                    return
                split(u + LEAD, (i + LEAD) % SLOTS)

            def chunk_hi(c, par, dst):
                act.wait_ge(c_ready, c + 1)
                act.activation(dst, a_buf[:, par, :], ACT.Copy).then_inc(c_hi_done, 1)

            def h_split(n, k):
                g = gain_col(n)
                act.activation(h_hi[:, k, :], X[:, k, :], ACT.Copy, scale=cols[:, bass.ds(g + k, 1)]).then_inc(h_hi_done, 1)

            split(0, 0)
            act.wait_ge(cols_done, 16)
            for k in range(KD):
                act.wait_ge(x_in_done[k // 2], 16)
                h_split(0, k)
            for u in range(1, LEAD):
                split(u, u)

            g_count = 0
            n_mem = 0
            kv = 0
            heads = 0
            for i_ph, (kind, layer, u0, t0, c0, part) in enumerate(phases):
                peel = i_ph == last_phase

                def mem_hi():
                    act.wait_ge(n_lo_done, n_mem * (KD + 1) + 1)
                    for k in range(KD):
                        act.activation(n_hi[:, k, :], mT[:, k, :], ACT.Copy,
                                       scale=cols[:, (layer * 5 + 3) * KD + k:(layer * 5 + 3) * KD + k + 1])\
                           .then_inc(n_hi_done, 1)

                if kind == "up":
                    def body(g):
                        for i in range(4):
                            ahead(u0 + 4 * g + i, i)
                            if i % 2:
                                p = 2 * g + i // 2
                                act.wait_ge(g_done, g_count + p + 1)
                                act.activation(t_buf[:, i // 2, :], g_buf[:, i // 2, :], ACT.Tanh, scale=0.5)\
                                   .then_inc(tanh_done, 1)
                                chunk_hi(c0 + p, i // 2, dst[:, p, :])
                    dst = f_hi if part == (0, KF) else m_hi
                    groups(act, (part[1] - part[0]) // 2, body, peel_first=(u0 == 0))
                    g_count += part[1] - part[0]
                elif kind == "down":
                    n = RESID.index(i_ph) + 1 if i_ph in RESID else None
                    per = 3 if part == (0, KF) else 1
                    if phases[i_ph + 1:] and phases[i_ph + 1][0] == "s5":
                        s5_matrices(act, 0)

                    def body(g):
                        for i in range(4 * per):
                            ahead(u0 + 4 * per * g + i, i)
                            if i % per == per - 1 and n in h_base:
                                k = 4 * g + i // per
                                act.wait_ge(tile_done, t0 + k + 1)
                                h_split(n, k)
                    groups(act, 2, body, peel_last=peel)
                elif kind == "conv_cv":
                    def body(g):
                        for i in range(4):
                            ahead(u0 + 4 * g + i, i)
                    groups(act, 4, body)
                    g_count += KD
                elif kind in ("conv_b", "q"):
                    def body(g):
                        for i in range(4):
                            ahead(u0 + 4 * g + i, i)
                            chunk_hi(c0 + 4 * g + i, i % 2, m_hi[:, 4 * g + i, :])
                    groups(act, 2, body)
                elif kind in ("conv_o", "o"):
                    n = RESID.index(i_ph) + 1

                    def body(g):
                        for i in range(4):
                            ahead(u0 + 4 * g + i, i)
                            k = 4 * g + i
                            act.wait_ge(tile_done, t0 + k + 1)
                            h_split(n, k)
                    if kind == "conv_o":
                        mem_hi()
                        n_mem += 1
                    groups(act, 2, body)
                elif kind == "glu":
                    n = RESID.index(i_ph) + 1

                    def body(g):
                        if isinstance(g, int):
                            mem_hi()
                        for i in range(4):
                            ahead(u0 + 4 * g + i, i)
                            if i % 2:
                                act.wait_ge(unit_done, u0 + 4 * g + i + 1)
                                act.activation(t_buf[:, i // 2, :], PS[:, i, :], ACT.Tanh, scale=0.25)\
                                   .then_inc(tanh_done, 1)
                                k = 2 * g + i // 2
                                act.wait_ge(tile_done, t0 + 2 * k + 2)
                                h_split(n, k)
                    groups(act, 4, body, peel_last=True)
                    n_mem += 1
                elif kind == "k":
                    def body(g):
                        for i in range(4):
                            ahead(u0 + 4 * g + i, i)
                            act.wait_ge(unit_done, u0 + 4 * g + i + 1)
                            act.activation(k_hi[:, 4 * g + i, :], PS[:, i, 0:MEM], ACT.Copy).then_inc(kv_hi_done, 1)
                    groups(act, 2, body)
                elif kind == "v":
                    for g in range(2):
                        for i in range(4):
                            ahead(u0 + 4 * g + i, i)
                        act.wait_ge(unit_done, u0 + 4 * g + 4)
                        for mc in range(2):
                            act.activation(v_hi[:, mc, g * 512:(g + 1) * 512], PS[:, 2 * g + mc, :], ACT.Copy)\
                               .then_inc(kv_hi_done, 1)
                elif kind == "core":
                    def exp(h):
                        act.wait_ge(bias_done, heads + h + 1)
                        for t in range(4):
                            ins = act.activation(prob[:, h % 2, t, :], PS[:, 2 * (h % 2) + t // 2, (t % 2) * MEM:(t % 2 + 1) * MEM],
                                                 ACT.Exp, bias=nb[:, h % 2, t:t + 1], scale=1.0 / 16,
                                                 accum_out=esum[:, h % 2, t:t + 1])
                        ins.then_inc(exp_done, 1)

                    def pt(h):
                        act.wait_ge(pt_done, heads + h + 1)
                        if h or heads:
                            act.wait_ge(pv_done, heads + h)
                        act.activation(pt_hi[:, :, :], PS[:, 4:6, :], ACT.Copy).then_inc(pt_hi_done, 1)

                    def o(h):
                        act.wait_ge(pv_done, heads + h + 1)
                        act.activation(m_hi[:, 2 * h:2 * h + 2, :], PS[:, 6:8, :], ACT.Copy).then_inc(o_hi_done, 1)

                    exp(0)
                    exp(1)
                    for h in range(HEADS):
                        pt(h)
                        if h + 2 < HEADS:
                            exp(h + 2)
                        o(h)
                    heads += HEADS
                elif kind == "s5":
                    def copy(o, a):
                        return act.activation(o, a, ACT.Copy)

                    def gelu(r):
                        for ch in range(2):
                            c = 2 * r + ch
                            act.wait_ge(y_arg, c + 1)
                            act.activation(t_buf[:, ch, :], u_buf[:, :], ACT.Tanh, scale=math.sqrt(2 / math.pi)).then_inc(y_tanh, 1)
                            act.wait_ge(c_ready, c0 + c + 1)
                            act.activation(by_step(m_hi[:, c, :]), a_buf[:, ch, :].rearrange("p (j n) -> p j n", j=DT_T), ACT.Copy)\
                               .then_inc(c_hi_done, 1)

                    act.wait_ge(s5_u, 2)
                    s5_u4(copy, 0, (0, 1)).then_inc(s5_u4a, 1)
                    for r in range(4):
                        if r < 3:
                            act.wait_ge(s5_u, 2 * r + 4)
                            act.wait_ge(s5_x, r + 1)
                            s5_u4(copy, r + 1, range(4)).then_inc(s5_u4a, 1)
                            s5_matrices(act, r + 1)
                        if r:
                            gelu(r - 1)
                        for ch in range(2):
                            c = 2 * r + ch
                            act.wait_ge(y_done, c + 1)
                            act.activation(t_buf[:, ch, :], g_buf[:, ch, :], ACT.Square, scale=math.sqrt(0.044715)).then_inc(y2_done, 1)
                        if r == 3:
                            gelu(r)

        def s5_vector(dve, i_ph, c0, norm):
            M, A, S = ALU.mult, ALU.add, ALU.subtract
            count = [0]

            def step(ins):
                ins.then_inc(s5_step, 1)
                count[0] += 1
                dve.wait_ge(s5_step, count[0])

            def op(o, a, b, f):
                step(dve.tensor_tensor(o, a, b, f))

            def u_of(r):
                for ch in range(2):
                    k = 2 * r + ch
                    dve.scalar_tensor_tensor(uq[:, r % 2, ch, :, :], by_step(X[:, k, :]), cols[:, g + k:g + k + 1],
                                             by_step(rstd[:, :]), M, M).then_inc(s5_u, 1)

            def gelu(r):
                for ch in range(2):
                    c = 2 * r + ch
                    y = g_buf[:, ch, :]
                    dve.wait_ge(y2_done, c + 1)
                    dve.scalar_tensor_tensor(u_buf[:, :], t_buf[:, ch, :], 1.0, y, A, M).then_inc(y_arg, 1)
                    dve.wait_ge(y_tanh, c + 1)
                    dve.scalar_tensor_tensor(a_buf[:, ch, :], t_buf[:, ch, :], 1.0, y, A, M).then_inc(c_ready, 1)
                for ch in range(2):
                    c = 2 * r + ch
                    dve.wait_ge(c_hi_done, c0 + c + 1)
                    dve.tensor_tensor(by_step(m_lo[:, c, :]), a_buf[:, ch, :].rearrange("p (j n) -> p j n", j=DT_T),
                                      by_step(m_hi[:, c, :]).bitcast(F32), S).then_inc(c_lo_done, 1)

            def halves(t):
                return t.rearrange("p (c q) n -> p c q n", c=2)

            norm("x", norm_of(i_ph), SEQ)
            g = gain_col(norm_of(i_ph))
            u_of(0)
            dve.wait_ge(s5_u, 2)
            s5_u4(dve.tensor_copy, 0, (2, 3)).then_inc(s5_u4v, 1)
            px = [PS[:, 0:4, :].rearrange("p q (c r n) -> p r c q n", c=2, r=2)[:, j] for j in range(2)]
            R = [halves(t[:, :, :]) for t in (r0, r1, r2, r3)]
            for r in range(4):
                rot = cut_stage(stage[r % 2])[2]
                cos, sin = (halves(rot[:, j, :, :]) for j in range(2))
                if r < 3:
                    if r:
                        dve.wait_ge(y_done, 2 * r)
                    u_of(r + 1)
                dve.wait_ge(stage_in[r % 2], 16 * (r // 2 + 1))
                dve.wait_ge(s5_x, r + 1)
                if r:
                    dve.wait_ge(s5_y, 2 * r)
                op(R[0], px[0], cos, M)
                op(R[1], px[1], sin, M)
                op(R[2], px[1], cos, M)
                dve.tensor_tensor(R[3], px[0], sin, M).then_inc(s5_xfree, 1)
                op(R[0], R[0], R[1], A)
                dve.wait_ge(s5_xfree, r + 1)
                op(R[2], R[2], R[3], S)
                for ch in range(2):
                    for i in range(4 * ch, 4 * ch + 4):
                        for t in (r0, r2):
                            step(dve.tensor_tensor_scan(t[:, i, :], mag4[:, QT * r + i:QT * r + i + 1].to_broadcast([P, NCH]),
                                                        t[:, i, :], 0.0, M, A))
                    z0, z1, z2, z3, co, si = (t[:, ch] for t in R + [cos, sin])
                    op(z1, z0, co, M)
                    op(z3, z2, si, M)
                    op(z1, z1, z3, S)
                    op(z0, z0, si, M)
                    op(z2, z2, co, M)
                    dve.tensor_tensor(z0, z0, z2, A).then_inc(s5_s, 1)
                if r:
                    gelu(r - 1)
                for ch in range(2):
                    c = 2 * r + ch
                    dve.wait_ge(s5_y, c + 1)
                    dve.scalar_tensor_tensor(g_buf[:, ch, :], uq[:, r % 2, ch, :, :].rearrange("p j n -> p (j n)"),
                                             cols[:, G_SKIP + c:G_SKIP + c + 1], PS[:, 5 + ch, :], M, A).then_inc(y_done, 1)
            gelu(3)

        @block.vector
        def _(dve):
            def split(u, slot):
                dve.wait_ge(w_hi_done, u + 1)
                dve.tensor_tensor(w_lo[:, slot, :], raw[:, slot, :], w_hi[:, slot, :].bitcast(F32), ALU.subtract)\
                   .then_inc(w_lo_done, 1)

            def ahead(u, i):
                if isinstance(u, int) and u + LEAD >= UNITS:
                    return
                split(u + LEAD, (i + LEAD) % SLOTS)

            def chunk_lo(c, par, dst, hi):
                dve.wait_ge(c_hi_done, c + 1)
                dve.tensor_tensor(dst, a_buf[:, par, :], hi.bitcast(F32), ALU.subtract).then_inc(c_lo_done, 1)

            def h_rest(n, k):
                dve.wait_ge(h_hi_done, h_base[n] + k + 1)
                dve.scalar_tensor_tensor(h_lo[:, k, :], X[:, k, :], cols[:, bass.ds(gain_col(n) + k, 1)],
                                         h_hi[:, k, :].bitcast(F32), ALU.mult, ALU.subtract).then_inc(h_lo_done, 1)

            nsteps = [0]

            def norm(kind, n, width):
                def step(ins):
                    ins.then_inc(newton, 1)
                    nsteps[0] += 1
                    dve.wait_ge(newton, nsteps[0])
                if kind == "x":
                    a, y, t = (small[:, j, :] for j in range(3))
                    sums = PS[:, NORM_BANK, 0:SEQ // P]
                else:
                    a, y, t = nt_a[:, 0:width], rstd[:, 0:width], u_buf[:, 0:width]
                    sums = PS[:, NORM_BANK, 0:width]
                dve.wait_ge(sum_done, ssq_index(kind, n) + 1)
                step(dve.tensor_scalar(a, sums, 1.0 / D, EPS, ALU.mult, ALU.add))
                step(dve.tensor_scalar(y.bitcast(I32), a.bitcast(I32), -0.5, float(0x5f3759df), ALU.mult, ALU.add))
                for _ in range(3):
                    step(dve.tensor_tensor(t, y, y, ALU.mult))
                    step(dve.scalar_tensor_tensor(t, t, -0.5, a, ALU.mult, ALU.mult))
                    step(dve.scalar_tensor_tensor(y, t, 1.5, y, ALU.add, ALU.mult))
                if kind == "x":
                    dve.tensor_tensor(nt_a[:, :].rearrange("p (t j) -> p t j", j=P), ident[:, None, :].to_broadcast([P, SEQ // P, P]),
                                      y[:, :, None].to_broadcast([P, SEQ // P, P]), ALU.mult).then_inc(diag_done, 1)
                    dve.wait_ge(spread_done, n + 1)
                    step(dve.tensor_copy(rstd[:, :], PS[:, NORM_BANK, :]))

            def mem_rest(layer, n_mem):
                norm("mem", layer, MEM)
                dve.tensor_tensor(mT[:, :, :], mT[:, :, :], rstd[:, None, 0:MEM].to_broadcast([P, KD, MEM]), ALU.mult)\
                   .then_inc(n_lo_done, 1)
                dve.wait_ge(n_lo_done, n_mem * (KD + 1) + 1)
                for k in range(KD):
                    dve.wait_ge(n_hi_done, n_mem * KD + k + 1)
                    g = (layer * 5 + 3) * KD + k
                    dve.scalar_tensor_tensor(n_lo[:, k, :], mT[:, k, :], cols[:, g:g + 1], n_hi[:, k, :].bitcast(F32),
                                             ALU.mult, ALU.subtract).then_inc(n_lo_done, 1)

            split(0, 0)
            dve.wait_ge(cols_done, 16)
            for k in range(KD):
                dve.wait_ge(x_in_done[k // 2], 16)
                h_rest(0, k)
            for u in range(1, LEAD):
                split(u, u)

            pairs = 0
            g_count = 0
            u_count = 0
            n_mem = 0
            kv = 0
            heads = 0
            for i_ph, (kind, layer, u0, t0, c0, part) in enumerate(phases):
                peel = i_ph == last_phase
                if kind == "up":
                    def body(g):
                        first = isinstance(g, int) and g == 0 and part[0] == 0
                        for i in range(4):
                            p = 2 * g + i // 2
                            b = i // 2
                            ahead(u0 + 4 * g + i, i)
                            if first and i == 0:
                                norm("x", norm_of(i_ph), SEQ)
                            dve.wait_ge(unit_done, u0 + 4 * g + i + 1)
                            if i % 2 == 0:
                                dve.tensor_tensor(g_buf[:, b, :], PS[:, i, :], rstd[:, :], ALU.mult).then_inc(g_done, 1)
                                dve.wait_ge(g_done, g_count + p + 1)
                                continue
                            dve.tensor_tensor(u_buf[:, :], PS[:, i, :], rstd[:, :], ALU.mult).then_inc(tile_done, 2)
                            dve.wait_ge(tile_done, t0 + 2 * p + 2)
                            dve.tensor_tensor(u_buf[:, :], u_buf[:, :], g_buf[:, b, :], ALU.mult).then_inc(u_done, 1)
                            dve.wait_ge(u_done, u_count + p + 1)
                            dve.wait_ge(tanh_done, pairs + p + 1)
                            dve.scalar_tensor_tensor(a_buf[:, b, :], t_buf[:, b, :], 1.0, u_buf[:, :], ALU.add, ALU.mult)\
                               .then_inc(c_ready, 1)
                            chunk_lo(c0 + p, b, lo[:, p, :], hi[:, p, :])
                    hi, lo = (f_hi, f_lo) if part == (0, KF) else (m_hi, m_lo)
                    n = part[1] - part[0]
                    groups(dve, n // 2, body, peel_first=(part[0] == 0))
                    pairs += n
                    g_count += n
                    u_count += n
                    if part == CUTS[0] and layer == 0:
                        dve.wait_ge(den_done, 1)
                        dve.reciprocal(tmp[:, 9, :], tmp[:, 8, :]).then_inc(rden_done, 1)
                elif kind == "down":
                    n = RESID.index(i_ph) + 1 if i_ph in RESID else None
                    per = 3 if part == (0, KF) else 1
                    if phases[i_ph + 1:] and phases[i_ph + 1][0] == "s5":
                        dve.memset(MB[:, :, :, :], 0.0).then_inc(s5_mb0, 1)

                    def body(g):
                        for i in range(4 * per):
                            ahead(u0 + 4 * per * g + i, i)
                            if i % per == per - 1:
                                k = 4 * g + i // per
                                dve.wait_ge(unit_done, u0 + 4 * per * g + i + 1)
                                dve.scalar_tensor_tensor(X[:, k, :], PS[:, i // per, :], 0.25, X[:, k, :], ALU.mult, ALU.add)\
                                   .then_inc(tile_done, 1)
                                if n in h_base:
                                    h_rest(n, k)
                    groups(dve, 2, body, peel_last=peel)
                elif kind == "conv_cv":
                    dve.memset(cu[:, :, 0:2], 0.0).then_inc(conv_step, 1)

                    def body(g):
                        first = isinstance(g, int) and g == 0
                        for i in range(4):
                            b = i // 2
                            ahead(u0 + 4 * g + i, i)
                            if first and i == 0:
                                norm("x", norm_of(i_ph), SEQ)
                            dve.wait_ge(unit_done, u0 + 4 * g + i + 1)
                            k = 2 * g + b
                            if i % 2 == 0:
                                dve.tensor_tensor(g_buf[:, b, :], PS[:, i, :], rstd[:, :], ALU.mult).then_inc(g_done, 1)
                                dve.wait_ge(g_done, g_count + k + 1)
                                continue
                            dve.tensor_tensor(u_buf[:, :], PS[:, i, :], rstd[:, :], ALU.mult).then_inc(tile_done, 2)
                            dve.wait_ge(tile_done, t0 + 2 * k + 2)
                            dve.tensor_tensor(cu[:, k, 2:2 + SEQ], u_buf[:, :], g_buf[:, b, :], ALU.mult).then_inc(u_done, 1)
                            dve.wait_ge(u_done, u_count + 2 * k + 1)
                            dve.wait_ge(conv_step, 1 + 2 * k)
                            col = G_CONV + k
                            dve.tensor_scalar(cv[:, k, :], cu[:, k, 0:SEQ], cols[:, bass.ds(col, 1)], None, ALU.mult)\
                               .then_inc(conv_step, 1)
                            dve.wait_ge(conv_step, 2 + 2 * k)
                            dve.scalar_tensor_tensor(cv[:, k, :], cu[:, k, 1:1 + SEQ], cols[:, bass.ds(col + KD, 1)],
                                                     cv[:, k, :], ALU.mult, ALU.add).then_inc(conv_step, 1)
                            dve.wait_ge(conv_step, 3 + 2 * k)
                            dve.scalar_tensor_tensor(cv[:, k, :], cu[:, k, 2:2 + SEQ], cols[:, bass.ds(col + 2 * KD, 1)],
                                                     cv[:, k, :], ALU.mult, ALU.add).then_inc(u_done, 1)
                            dve.wait_ge(u_done, u_count + 2 * k + 2)
                    groups(dve, 4, body, peel_first=True)
                    g_count += KD
                    u_count += 2 * KD
                elif kind in ("conv_b", "q"):
                    def body(g):
                        first = isinstance(g, int) and g == 0
                        for i in range(4):
                            k = 4 * g + i
                            ahead(u0 + 4 * g + i, i)
                            dve.wait_ge(unit_done, u0 + 4 * g + i + 1)
                            if kind == "q":
                                dve.tensor_tensor(a_buf[:, i % 2, :], PS[:, i, :], rstd[:, :], ALU.mult).then_inc(tile_done, 1)
                                dve.wait_ge(tile_done, t0 + k + 1)
                                dve.sem_inc(c_ready, 1)
                            else:
                                dve.tensor_tensor(u_buf[:, :], PS[:, i, :], rstd[:, :], ALU.mult).then_inc(tile_done, 1)
                                dve.wait_ge(tile_done, t0 + k + 1)
                                dve.tensor_tensor(a_buf[:, i % 2, :], u_buf[:, :], cv[:, k, :], ALU.mult).then_inc(c_ready, 1)
                            chunk_lo(c0 + k, i % 2, m_lo[:, k, :], m_hi[:, k, :])
                    groups(dve, 2, body)
                elif kind in ("conv_o", "o"):
                    n = RESID.index(i_ph) + 1

                    def body(g):
                        for i in range(4):
                            k = 4 * g + i
                            ahead(u0 + 4 * g + i, i)
                            dve.wait_ge(unit_done, u0 + 4 * g + i + 1)
                            dve.tensor_tensor(X[:, k, :], PS[:, i, :], X[:, k, :], ALU.add).then_inc(tile_done, 1)
                            h_rest(n, k)
                    if kind == "conv_o":
                        mem_rest(layer, n_mem)
                        n_mem += 1
                    groups(dve, 2, body)
                elif kind == "glu":
                    n = RESID.index(i_ph) + 1

                    def body(g):
                        if isinstance(g, int):
                            mem_rest(layer, n_mem)
                        for i in range(4):
                            ahead(u0 + 4 * g + i, i)
                            if i % 2:
                                k = 2 * g + i // 2
                                b = i // 2
                                dve.wait_ge(unit_done, u0 + 4 * g + i + 1)
                                dve.wait_ge(tanh_done, pairs + k + 1)
                                dve.scalar_tensor_tensor(u_buf[:, :], t_buf[:, b, :], 1.0, PS[:, i - 1, :], ALU.add, ALU.mult)\
                                   .then_inc(u_done, 1)
                                dve.wait_ge(u_done, u_count + k + 1)
                                dve.scalar_tensor_tensor(X[:, k, :], u_buf[:, :], 0.25, X[:, k, :], ALU.mult, ALU.add)\
                                   .then_inc(tile_done, 2)
                                h_rest(n, k)
                    groups(dve, 4, body, peel_last=True)
                    n_mem += 1
                    pairs += KD
                    u_count += KD
                elif kind == "k":
                    def body(g):
                        first = isinstance(g, int) and g == 0
                        for i in range(4):
                            k = 4 * g + i
                            ahead(u0 + 4 * g + i, i)
                            if first and i == 1:
                                norm("x", norm_of(i_ph), SEQ)
                            dve.wait_ge(kv_hi_done, kv + k + 1)
                            dve.tensor_tensor(k_lo[:, k, :], PS[:, i, 0:MEM], k_hi[:, k, :].bitcast(F32), ALU.subtract)\
                               .then_inc(tile_done, 1)
                    groups(dve, 2, body, peel_first=True)
                    kv += KD
                elif kind == "v":
                    for g in range(2):
                        for i in range(4):
                            ahead(u0 + 4 * g + i, i)
                        for mc in range(2):
                            dve.wait_ge(kv_hi_done, kv + 2 * g + mc + 1)
                            s = slice(g * 512, (g + 1) * 512)
                            dve.tensor_tensor(v_lo[:, mc, s], PS[:, 2 * g + mc, :], v_hi[:, mc, s].bitcast(F32), ALU.subtract)\
                               .then_inc(tile_done, 1)
                    kv += 4
                elif kind == "core":
                    def bias(h):
                        dve.wait_ge(score_done, heads + h + 1)
                        b = 2 * (h % 2)
                        dve.tensor_reduce(mx[:, h % 2, :], PS[:, b:b + 2, :].rearrange("p b (t m) -> p (b t) m", t=2), AX.X, ALU.max)\
                           .then_inc(att_step, 1)
                        att_n[0] += 1
                        dve.wait_ge(att_step, att_n[0])
                        dve.tensor_scalar(nb[:, h % 2, :], mx[:, h % 2, :], -1.0 / 16, None, ALU.mult).then_inc(bias_done, 1)

                    def normalise(h):
                        dve.wait_ge(exp_done, heads + h + 1)
                        dve.reciprocal(rsum[:, h % 2, :], esum[:, h % 2, :]).then_inc(att_step, 1)
                        att_n[0] += 1
                        dve.wait_ge(att_step, att_n[0])
                        for t in range(4):
                            ins = dve.tensor_scalar(prob[:, h % 2, t, :], prob[:, h % 2, t, :], rsum[:, h % 2, t:t + 1], None, ALU.mult)
                        ins.then_inc(prob_done, 1)

                    def pt(h):
                        dve.wait_ge(pt_hi_done, heads + h + 1)
                        dve.tensor_tensor(pt_lo[:, :, :], PS[:, 4:6, :], pt_hi[:, :, :].bitcast(F32), ALU.subtract).then_inc(pt_lo_done, 1)

                    def o(h):
                        dve.wait_ge(o_hi_done, heads + h + 1)
                        s = slice(2 * h, 2 * h + 2)
                        dve.tensor_tensor(m_lo[:, s, :], PS[:, 6:8, :], m_hi[:, s, :].bitcast(F32), ALU.subtract).then_inc(o_lo_done, 1)

                    att_n = [2 * heads]
                    bias(0)
                    bias(1)
                    normalise(0)
                    for h in range(HEADS):
                        pt(h)
                        if h + 1 < HEADS:
                            normalise(h + 1)
                        if h + 2 < HEADS:
                            bias(h + 2)
                        o(h)
                    heads += HEADS
                elif kind == "s5":
                    s5_vector(dve, i_ph, c0, norm)
            norm("x", len(RESID), SEQ)
            for k in range(KD):
                dve.scalar_tensor_tensor(X[:, k, :], X[:, k, :], cols[:, G_FINAL + k:G_FINAL + k + 1], rstd[:, :], ALU.mult, ALU.mult)\
                   .then_inc(fin, 1)

        def s5_turn(te, r):
            E, F, _ = cut_stage(stage[r % 2])
            te.wait_ge(stage_in[r % 2], 16 * (r // 2 + 1))
            if r:
                te.wait_ge(s5_et, 5 * r)
            for b in range(4):
                if b >= 2:
                    te.wait_ge(s5_et, 5 * r + b - 1)
                for j in range(4):
                    i = 4 * (b % 2) + j
                    mm = te.transpose(PS[:, s5_bank(b), j * P:(j + 1) * P], E[:, b // 2, :, i, :], ident[:, :])
                mm.then_inc(s5_tr, 1)
            te.wait_ge(s5_et, 5 * r + 3)
            for ch in range(2):
                for part_, start in ((0, True), (1, False)):
                    for q in range(4):
                        i = 4 * ch + q
                        mm = te.matmul(PS[32 * q:32 * q + 32, s5_bank(4), ch * P:(ch + 1) * P], E[:, part_, 0, i, :],
                                       F[:, part_, 0:4, i, :], start=start, stop=not start, skip_group_check=True)
            mm.then_inc(s5_tr, 1)

        def s5_inputs(te, r):
            te.wait_ge(s5_et, 5 * r + 4)
            te.wait_ge(s5_u4a, r + 1)
            if r == 0:
                te.wait_ge(s5_u4v, 1)
            for i in range(QT):
                for ri in range(2):
                    c = 2 * (i // 4) + ri
                    mm = te.matmul(PS[:, i % 4, c * P:(c + 1) * P], ET[:, ri, i, :], u4[:, i, :], start=True, stop=True,
                                   skip_group_check=True)
            mm.then_inc(s5_x, 1)

        def s5_within(te, r):
            te.wait_ge(s5_et, 5 * r + 5)
            if r:
                te.wait_ge(y_done, 2 * r)
            for ch in range(2):
                for l in range(DT_T):
                    te.matmul(PS[:, 5 + ch, l * NCH:], MB[:, ch, l, :], uq[:, r % 2, ch, 0:DT_T - l, :], start=l == 0, stop=False,
                              skip_group_check=True)

        def s5_outputs(te, r):
            F = cut_stage(stage[r % 2])[1]
            for ch in range(2):
                te.wait_ge(s5_s, 2 * r + ch + 1)
                for j in range(DT_T):
                    for ri, state in ((0, r1), (1, r0)):
                        for q in range(4):
                            i = 4 * ch + q
                            mm = te.matmul(PS[32 * q:32 * q + 32, 5 + ch, j * NCH + 1:(j + 1) * NCH], F[:, ri, j + 1, i, :],
                                           state[:, i, 0:NCH - 1], start=False, stop=ri == 1 and j == DT_T - 1, skip_group_check=True)
                mm.then_inc(s5_y, 1)

        @block.tensor
        def _(te):
            def three(ps, whi, wlo, xhi, xlo, start, stop):
                te.matmul(ps, whi, xhi, start=start, stop=False)
                te.matmul(ps, whi, xlo, start=False, stop=False)
                return te.matmul(ps, wlo, xhi, start=False, stop=stop)

            def unit(u, slot, bank, ks, xh, xl, start, stop, ready=None, width=SEQ):
                te.wait_ge(w_lo_done, u + 1)
                for t, k in enumerate(ks):
                    if ready:
                        ready(k)
                    s = slice(t * P, (t + 1) * P)
                    mm = three(PS[:, bank, 0:width], w_hi[:, slot, s], w_lo[:, slot, s], xh[:, k, :], xl[:, k, :],
                               start and t == 0, stop and t == len(ks) - 1)
                mm.then_inc(unit_done, 1)

            def bank_free(t):
                if not (isinstance(t, int) and t < 4):
                    te.wait_ge(tile_done, t - 3)

            def sums(kind, n, width):
                te.wait_ge(ssq_done, ssq_index(kind, n) + 1)
                if ssq_index(kind, n) == 0:
                    te.wait_ge(const_done, 2)
                if kind == "x":
                    for t in range(SEQ // P):
                        mm = te.matmul(PS[:, NORM_BANK, t:t + 1], ssq[:, t * P:(t + 1) * P], ones[:, 0:1], start=True, stop=True,
                                       skip_group_check=True)
                    mm.then_inc(sum_done, 1)
                else:
                    te.matmul(PS[:, NORM_BANK, 0:width], ones[:, :], ssq[:, 0:width], start=True, stop=True).then_inc(sum_done, 1)

            def spread(n):
                te.wait_ge(diag_done, n + 1)
                te.matmul(PS[:, NORM_BANK, :], ones[:, :], nt_a[:, :], start=True, stop=True).then_inc(spread_done, 1)

            heads = 0
            n_mem = 0
            for i_ph, (kind, layer, u0, t0, c0, part) in enumerate(phases):
                n = norm_of(i_ph)
                if kind in ("up", "conv_cv"):
                    def body(g):
                        first = isinstance(g, int) and g == 0 and (kind != "up" or part[0] == 0)
                        for i in range(4):
                            bank_free(t0 + 4 * g + i)
                            ready = (lambda k: te.wait_ge(h_lo_done, h_base[n] + k + 1)) if first and i == 0 else None
                            unit(u0 + 4 * g + i, i, i, range(KD), h_hi, h_lo, True, True, ready)
                            if first and i == (n == 0):
                                sums("x", n, SEQ)
                            if first and i == (n == 0) + 1:
                                spread(n)
                    groups(te, (part[1] - part[0] if kind == "up" else KD) // 2, body,
                           peel_first=(kind != "up" or part[0] == 0))
                elif kind == "down":
                    if phases[i_ph + 1:] and phases[i_ph + 1][0] == "s5":
                        s5_turn(te, 0)
                    te.wait_ge(c_lo_done, c0 - 1)

                    def body(g):
                        for j in range(4):
                            bank_free(t0 + 4 * g + j)
                            last = (lambda k: te.wait_ge(c_lo_done, c0) if k == part[1] - part[0] - 1 else None) if j == 0 else None
                            if part == (0, KF):
                                for c, (a, b) in enumerate(CUTS):
                                    i = 3 * j + c
                                    unit(u0 + 12 * g + i, i % SLOTS, j, range(a, b), f_hi, f_lo, c == 0, c == 2, last)
                            else:
                                unit(u0 + 4 * g + j, j, j, range(part[1] - part[0]), m_hi, m_lo, True, True, last)
                    groups(te, 2, body)
                elif kind == "conv_b":
                    def body(g):
                        for i in range(4):
                            bank_free(t0 + 4 * g + i)
                            unit(u0 + 4 * g + i, i, i, range(KD), h_hi, h_lo, True, True)
                    groups(te, 2, body)
                elif kind in ("conv_o", "o"):
                    if kind == "conv_o":
                        sums("mem", layer, MEM)

                    def body(g):
                        first = isinstance(g, int) and g == 0
                        for i in range(4):
                            bank_free(t0 + 4 * g + i)
                            ready = None
                            if first and i == 0:
                                ready = (lambda k: te.wait_ge(c_lo_done, c0 - KD + k + 1)) if kind == "conv_o" else \
                                        (lambda k: te.wait_ge(o_lo_done, heads - HEADS + k // 2 + 1))
                            unit(u0 + 4 * g + i, i, i, range(KD), m_hi, m_lo, True, True, ready)
                    groups(te, 2, body, peel_first=True)
                elif kind == "glu":
                    def body(g):
                        if isinstance(g, int) and g:
                            sums("mem", layer, MEM)
                        for i in range(4):
                            bank_free(t0 + 4 * g + i)
                            ready = (lambda k: te.wait_ge(c_lo_done, c0 - KD + k + 1)) if isinstance(g, int) and g + i == 0 else None
                            unit(u0 + 4 * g + i, i, i, range(KD), m_hi, m_lo, True, True, ready)
                    groups(te, 4, body, peel_first=True, peel_last=True)
                elif kind == "k":
                    te.wait_ge(n_lo_done, (n_mem + 1) * (KD + 1))
                    n_mem += 1

                    def body(g):
                        for i in range(4):
                            bank_free(t0 + 4 * g + i)
                            unit(u0 + 4 * g + i, i, i, range(KD), n_hi, n_lo, True, True, width=MEM)
                            if isinstance(g, int) and g == 0 and i == 0:
                                sums("x", n, SEQ)
                            if isinstance(g, int) and g == 0 and i == 2:
                                spread(n)
                    groups(te, 2, body, peel_first=True)
                elif kind == "v":
                    for g in range(2):
                        bank_free(t0 + 2 * g + 1)
                        for i in range(4):
                            te.wait_ge(w_lo_done, u0 + 4 * g + i + 1)
                            for kk in range(2):
                                k = 2 * i + kk
                                s = slice(kk * 512, (kk + 1) * 512)
                                for mc in range(2):
                                    ms = slice(mc * P, (mc + 1) * P)
                                    mm = three(PS[:, 2 * g + mc, :], n_hi[:, k, ms], n_lo[:, k, ms], w_hi[:, i, s], w_lo[:, i, s],
                                               k == 0, k == KD - 1)
                            mm.then_inc(unit_done, 1)
                elif kind == "q":
                    def body(g):
                        for i in range(4):
                            bank_free(t0 + 4 * g + i)
                            ready = None
                            unit(u0 + 4 * g + i, i, i, range(KD), h_hi, h_lo, True, True)
                    te.wait_ge(h_lo_done, h_base[n] + KD)
                    groups(te, 2, body)
                elif kind == "core":
                    te.wait_ge(c_lo_done, c0)
                    te.wait_ge(tile_done, t0)

                    def scores(h):
                        if h >= 2:
                            te.wait_ge(exp_done, heads + h - 1)
                        for t in range(4):
                            out_ = PS[:, 2 * (h % 2) + t // 2, (t % 2) * MEM:(t % 2 + 1) * MEM]
                            ts_ = slice(t * P, (t + 1) * P)
                            for dc in range(2):
                                k = 2 * h + dc
                                mm = three(out_, m_hi[:, k, ts_], m_lo[:, k, ts_], k_hi[:, k, :], k_lo[:, k, :], dc == 0, dc == 1)
                        mm.then_inc(score_done, 1)

                    def turn(h):
                        te.wait_ge(prob_done, heads + h + 1)
                        if h or heads:
                            te.wait_ge(pt_lo_done, heads + h)
                        for mc in range(2):
                            for t in range(4):
                                mm = te.transpose(PS[:, 4 + mc, t * P:(t + 1) * P], prob[:, h % 2, t, mc * P:(mc + 1) * P], ident[:, :])
                        mm.then_inc(pt_done, 1)

                    def values(h):
                        te.wait_ge(pt_lo_done, heads + h + 1)
                        if h or heads:
                            te.wait_ge(o_lo_done, heads + h)
                        for dc in range(2):
                            s = slice(h * HD + dc * P, h * HD + (dc + 1) * P)
                            for mc in range(2):
                                mm = three(PS[:, 6 + dc, :], v_hi[:, mc, s], v_lo[:, mc, s], pt_hi[:, mc, :], pt_lo[:, mc, :],
                                           mc == 0, mc == 1)
                        mm.then_inc(pv_done, 1)

                    scores(0)
                    scores(1)
                    for h in range(HEADS):
                        turn(h)
                        if h + 2 < HEADS:
                            scores(h + 2)
                        values(h)
                    heads += HEADS
                elif kind == "s5":
                    te.wait_ge(s5_et, 4)
                    sums("x", n, SEQ)
                    spread(n)
                    te.wait_ge(tile_done, t0)
                    s5_inputs(te, 0)
                    for r in range(4):
                        s5_within(te, r)
                        if r < 3:
                            s5_turn(te, r + 1)
                            te.wait_ge(s5_xfree, r + 1)
                            s5_inputs(te, r + 1)
                        s5_outputs(te, r)
            sums("x", len(RESID), SEQ)
            spread(len(RESID))



def kernel(x, mem, norm_g, final_g, ffn1_up, ffn1_down, ffn2_up, ffn2_down, conv_w_in, conv_w, conv_w_out,
           ssm_a_re, ssm_a_im, ssm_log_dt, ssm_b_re, ssm_b_im, ssm_c_re, ssm_c_im, ssm_d, ssm_w_glu,
           xa_w_q, xa_w_kv, xa_w_o):
    import numpy as np
    import concourse.bacc as bacc
    from concourse.bass_utils import run_bass_kernel_spmd

    arr = {k: np.asarray(v) for k, v in locals().items() if k not in ("np", "bacc", "run_bass_kernel_spmd")}

    def chunks(a):
        a = np.asarray(a)
        return np.ascontiguousarray(a.reshape(a.shape[0], -1, P).transpose(2, 1, 0))

    def units(w):
        k, m = w.shape
        return w.reshape(k // P, P, m // P, P).transpose(2, 1, 0, 3).reshape(m // P, P, k)

    def paired(a, b):
        return np.stack([units(a), units(b)], 1).reshape(-1, P, D)

    def moving(w):
        return w.reshape(4, 2, P, 2, 512).transpose(3, 0, 2, 1, 4).reshape(8, P, D)

    stream, down = [], []
    for l in range(DEPTH):
        up1, up2 = arr["ffn1_up"][l], arr["ffn2_up"][l]
        stream.append(paired(up1[:, :FF], up1[:, FF:]))
        down.append(units(arr["ffn1_down"][l]))
        if l % 2 == 0:
            w = arr["conv_w_in"][l // 2]
            stream += [paired(w[:, :D], w[:, 2 * D:]), units(w[:, D:2 * D]), units(arr["conv_w_out"][l // 2])]
        else:
            w = arr["ssm_w_glu"][l // 2]
            stream.append(paired(w[:, :D], w[:, D:]))
        kv = arr["xa_w_kv"][l]
        stream += [units(kv[:, :D]), moving(kv[:, D:]), units(arr["xa_w_q"][l]), units(arr["xa_w_o"][l])]
        stream.append(paired(up2[:, :FF], up2[:, FF:]))
        down.append(units(arr["ffn2_down"][l]))

    def col(v):
        return v.reshape(-1, KD, P).transpose(2, 0, 1).reshape(P, -1)

    cols = np.concatenate([col(arr["norm_g"]), col(arr["final_g"]), col(arr["conv_w"][0]), col(arr["ssm_d"])], 1)

    def states(v):
        return v.reshape(NT, P).T

    s5p = np.stack([states(arr["ssm_a_re"][0]), states(arr["ssm_a_im"][0]),
                    states(np.broadcast_to(arr["ssm_log_dt"][0][:, None], (64, 64)))], 1)

    def blocks(v):
        v = v.reshape(NT, 2, 64, 16)
        b = np.zeros((2, 64, NT, 2, 16), np.float32)
        for g in range(2):
            b[g, :, :, g, :] = v[:, g].transpose(1, 0, 2)
        return b.reshape(P, NT, 32)

    bc = np.stack([blocks(arr["ssm_b_re"][0]), blocks(arr["ssm_b_im"][0]),
                   blocks(arr["ssm_c_re"][0].transpose(0, 2, 1)), blocks(arr["ssm_c_im"][0].transpose(0, 2, 1))], 1)
    bc = bc.reshape(P, 4, 4, QT * 32).transpose(2, 0, 1, 3)

    ins = {"x_in": chunks(arr["x"][0]), "mem_in": chunks(arr["mem"][0]), "cols_in": cols,
           "w8": np.concatenate(stream), "wd": np.concatenate(down), "s5p": s5p, "s5bc": bc}
    ins = {k: np.ascontiguousarray(v) for k, v in ins.items()}
    nc = bacc.Bacc("TRN2", target_bir_lowering=False, num_devices=1)
    aps = [nc.dram_tensor(k, v.shape, F32, kind="ExternalInput").ap() for k, v in ins.items()]
    out = nc.dram_tensor("out", (P, KD, SEQ), F32, kind="ExternalOutput").ap()
    scratch = nc.dram_tensor("scratch", (4, P, 26 * QT * 32), F32, kind="Internal").ap()
    build(nc, *aps, scratch, out)
    r = run_bass_kernel_spmd(nc, [ins], core_ids=[0])
    return r.results[0]["out"].transpose(2, 1, 0).reshape(1, SEQ, D)
```

```python
import math
from contextlib import ExitStack

import concourse.bass as bass
from concourse import mybir

ALU = mybir.AluOpType
ACT = mybir.ActivationFunctionType
AX = mybir.AxisListType
F32 = mybir.dt.float32
F32R = mybir.dt.float32r
I32 = mybir.dt.int32

P = 128
D = 1024
KD = D // P
SEQ = 512
MEM = 256
FF = 2816
KF = FF // P
DEPTH = 2
HEADS = 4
HD = D // HEADS
SLOTS = 4
LEAD = 3
UT = 8
EPS = 1e-6
DT_T = 4
NCH = SEQ // DT_T
QT = 8
NT = 32
G_FINAL = DEPTH * 5 * KD
G_CONV = G_FINAL + KD
G_SKIP = G_CONV + 3 * KD
NCOLS = G_SKIP + KD


def cut(x, bits, parts):
    out = []
    for _ in range(parts):
        m, e = math.frexp(x)
        out.append(math.ldexp(round(math.ldexp(m, bits)), e - bits))
        x -= out[-1]
    return out


TWO_PI = cut(2 * math.pi, 9, 4)
MAGIC = 12582912.0


VEC_SQ = 3
CUTS = [(0, 8), (8, 16), (16, KF)]


def plan():
    phases, u, t, c = [], 0, 0, 0
    sizes = {"conv_cv": (2 * KD, 2 * KD, 0), "conv_b": (KD, KD, KD), "conv_o": (KD, KD, 0), "s5": (0, 0, KD),
             "glu": (2 * KD, 2 * KD, 0), "k": (KD, KD, 0), "q": (KD, KD, KD), "core": (8, 4, 0), "o": (KD, KD, 0)}
    for layer in range(DEPTH):
        mixer = ["conv_cv", "conv_b", "conv_o"] if layer % 2 == 0 else ["s5", "glu"]
        for kind in ["ffn1"] + mixer + ["k", "q", "core", "o", "ffn2"]:
            if kind[:3] != "ffn":
                todo = [(kind, None, sizes[kind])]
            elif (kind, layer) in (("ffn2", 0), ("ffn1", 1)):
                todo = []
                for f0, f1 in CUTS:
                    n = f1 - f0
                    todo += [("up", (f0, f1), (2 * n, 2 * n, n)), ("down", (f0, f1), (KD, KD, 0))]
            else:
                todo = [("up", (0, KF), (2 * KF, 2 * KF, KF)), ("down", (0, KF), (3 * KD, KD, 0))]
            for name, part, (du, dt, dc) in todo:
                phases.append((name, layer, u, t, c, part))
                u, t, c = u + du, t + dt, c + dc
    return phases, u


def build(nc, x_in, mem_in, cols_in, w8, wd, s5p, s5bc, scratch, out):
    phases, UNITS = plan()
    RESID = [i for i, ph in enumerate(phases) if ph[0] in ("conv_o", "glu", "o") or ph[0] == "down" and ph[5][1] == KF]

    def norm_of(i):
        return 1 + max([n for n, r in enumerate(RESID) if r < i], default=-1)

    def gain_col(n):
        if n == len(RESID):
            return G_FINAL
        nxt = phases[RESID[n - 1] + 1] if n else phases[0]
        which = {"conv_cv": 1, "s5": 1, "k": 2, "up": 0 if n % 4 == 0 else 4}[nxt[0]]
        return (nxt[1] * 5 + which) * KD

    deferred = [n for n in range(len(RESID) + 1) if n < len(RESID) and not (n and phases[RESID[n - 1] + 1][0] == "s5")]
    at_once = [n for n in range(1, len(RESID) + 1) if n not in deferred]
    h_base = {n: KD * k for k, n in enumerate(deferred)}

    with ExitStack() as ctx:
        def sem(name):
            return ctx.enter_context(nc.semaphore(name))

        top = [(nc.sbuf_base + 31) // 32 * 32]

        def at(name, shape, dt, offset):
            return nc.alloc_sbuf_tensor_at(name, shape, dt, offset=offset)

        def size(shape):
            n = 4
            for s in shape[1:]:
                n *= s
            return (n + 31) // 32 * 32

        def sb(name, shape, dt=F32):
            t = at(name, shape, dt, top[0])
            top[0] += size(shape)
            assert top[0] <= nc.sbuf_usable_end, (name, top[0])
            return t

        X = sb("X", [P, KD, SEQ])
        h_at = top[0]
        h_hi = sb("h_hi", [P, KD, SEQ], F32R)
        h_lo = sb("h_lo", [P, KD, SEQ], F32R)
        raw = sb("raw", [P, SLOTS, UT * P])
        w_hi = sb("w_hi", [P, SLOTS, UT * P], F32R)
        w_lo = sb("w_lo", [P, SLOTS, UT * P], F32R)
        g_buf = sb("g_buf", [P, 2, SEQ])
        t_buf = sb("t_buf", [P, 2, SEQ])
        u_buf = sb("u_buf", [P, SEQ])
        a_buf = sb("a_buf", [P, 2, SEQ])
        rstd = sb("rstd", [P, SEQ])
        nt_a = sb("nt_a", [P, SEQ])
        small = sb("small", [P, 3, SEQ // P])
        sq_at = top[0]
        sq = sb("sq", [P, SEQ])
        ssq = sb("ssq", [P, SEQ])
        ident = sb("ident", [P, P])
        ones = sb("ones", [P, P])
        cols = sb("cols", [P, NCOLS])
        mx = sb("mx", [P, 2, 4])
        nb = sb("nb", [P, 2, 4])
        esum = sb("esum", [P, 2, 4])
        rsum = sb("rsum", [P, 2, 4])

        area = top[0]

        class Area:
            def __init__(self, start):
                self.at = start

            def take(self, name, shape, dt=F32):
                t = at(name, shape, dt, self.at)
                self.at += size(shape)
                assert self.at <= nc.sbuf_usable_end, (name, self.at)
                return t

        ffn = Area(area)
        f_hi = ffn.take("f_hi", [P, KF, SEQ], F32R)
        f_lo = ffn.take("f_lo", [P, KF, SEQ], F32R)
        mid = Area(area)
        m_hi = mid.take("m_hi", [P, KD, SEQ], F32R)
        u_at = mid.at
        m_lo = mid.take("m_lo", [P, KD, SEQ], F32R)
        conv = Area(mid.at)
        cu = conv.take("cu", [P, KD, SEQ + 2])
        cv = conv.take("cv", [P, KD, SEQ])
        att = Area(mid.at)
        k_hi = att.take("k_hi", [P, KD, MEM], F32R)
        k_lo = att.take("k_lo", [P, KD, MEM], F32R)
        v_hi = att.take("v_hi", [P, 2, D], F32R)
        v_lo = att.take("v_lo", [P, 2, D], F32R)
        mem_at = max(att.at, conv.at)
        ma = Area(mem_at)
        n_hi = ma.take("n_hi", [P, KD, MEM], F32R)
        n_lo = ma.take("n_lo", [P, KD, MEM], F32R)
        mT = ma.take("mT", [P, KD, MEM])
        mb = Area(mem_at)
        pt_hi = mb.take("pt_hi", [P, 2, SEQ], F32R)
        pt_lo = mb.take("pt_lo", [P, 2, SEQ], F32R)
        prob = at("prob", [P, 2, 4, MEM], F32, mem_at + 2 * size([P, KD, MEM]))
        STAGE = 26 * QT * 32
        s5 = Area(mid.at)
        mag4 = s5.take("mag4", [P, NT])
        prep = Area(s5.at + 4 * STAGE)
        stage = [s5.take(f"stage{i}", [P, STAGE]) for i in range(2)]

        def cut_stage(t):
            e, f = 8 * QT * 32, 18 * QT * 32
            return (t[:, 0:e].rearrange("p (r i k s) -> p r k i s", r=2, i=QT, k=4), t[:, e:f].rearrange("p (r k i s) -> p r k i s", r=2, k=5, i=QT),
                    t[:, f:].rearrange("p (r i n) -> p r i n", r=2, i=QT))
        pin = prep.take("pin", [P, 3, NT])
        tmp = prep.take("tmp", [P, 12, NT])
        tmpi = prep.take("tmpi", [P, NT], I32)
        pw = prep.take("pw", [P, 2, 5, NT])
        un = prep.take("un", [P, 2, 7, NT])
        coef = prep.take("coef", [P, 2, NT])
        bcq = prep.take("bcq", [P, 4, QT * 32])
        w0 = prep.take("w0", [P, 4 * QT * 32])
        w1 = prep.take("w1", [P, 4 * QT * 32])
        u_all = at("u_all", [P, KD, DT_T, NCH], F32, u_at)
        u4 = at("u4", [P, QT, NCH], F32, sq_at)
        s5h = Area(h_at)
        ET = s5h.take("ET", [P, 2, 2, QT, P])
        r0 = s5h.take("r0", [P, QT, NCH])
        r1 = s5h.take("r1", [P, QT, NCH])
        r2 = s5h.take("r2", [P, QT, NCH])
        r3 = s5h.take("r3", [P, QT, NCH])
        assert s5h.at <= h_at + 2 * size([P, KD, SEQ])
        MB = s5.take("MB", [P, 2, 4, P])

        PS = ctx.enter_context(nc.psum_tensor("PS", [P, 8, 512], F32))
        NORM_BANK = 4

        raw_in = [sem(f"raw_in{i}") for i in range(SLOTS)]
        w_hi_done = sem("w_hi_done")
        w_lo_done = sem("w_lo_done")
        unit_done = sem("unit_done")
        tile_done = sem("tile_done")
        x_in_done = [sem(f"x_in_done{i}") for i in range(4)]
        cols_done = sem("cols_done")
        mem_done = sem("mem_done")
        s5p_done = sem("s5p_done")
        bc_done = sem("bc_done")
        spilled = sem("spilled")
        e_in = [sem(f"e_in{i}") for i in range(2)]
        f_in = [sem(f"f_in{i}") for i in range(2)]
        out_done = sem("out_done")
        const_done = sem("const_done")
        ident0 = sem("ident0")
        h_hi_done = sem("h_hi_done")
        h_lo_done = sem("h_lo_done")
        sq_done = sem("sq_done")
        sq0_done = sem("sq0_done")
        sq_last_done = sem("sq_last_done")
        ssq_done = sem("ssq_done")
        sum_done = sem("sum_done")
        newton = sem("newton")
        diag_done = sem("diag_done")
        spread_done = sem("spread_done")
        g_done = sem("g_done")
        tanh_done = sem("tanh_done")
        u_done = sem("u_done")
        c_ready = sem("c_ready")
        c_hi_done = sem("c_hi_done")
        c_lo_done = sem("c_lo_done")
        kv_hi_done = sem("kv_hi_done")
        n_hi_done = sem("n_hi_done")
        n_lo_done = sem("n_lo_done")
        conv_step = sem("conv_step")
        score_done = sem("score_done")
        bias_done = sem("bias_done")
        att_step = sem("att_step")
        exp_done = sem("exp_done")
        prob_done = sem("prob_done")
        pt_done = sem("pt_done")
        pt_hi_done = sem("pt_hi_done")
        pt_lo_done = sem("pt_lo_done")
        pv_done = sem("pv_done")
        o_hi_done = sem("o_hi_done")
        o_lo_done = sem("o_lo_done")
        prep_step = sem("prep_step")
        den_done = sem("den_done")
        rden_done = sem("rden_done")
        s5_step = sem("s5_step")
        s5_tr = sem("s5_tr")
        s5_et = sem("s5_et")
        s5_lag = sem("s5_lag")
        s5_mb = sem("s5_mb")
        s5_mb0 = sem("s5_mb0")
        s5_u = sem("s5_u")
        s5_u4a = sem("s5_u4a")
        s5_u4v = sem("s5_u4v")
        s5_x = sem("s5_x")
        s5_xfree = sem("s5_xfree")
        s5_scan = sem("s5_scan")
        s5_z0 = sem("s5_z0")
        s5_re = sem("s5_re")
        s5_im = sem("s5_im")
        s5_prod = sem("s5_prod")
        s5_y = sem("s5_y")
        y_done = sem("y_done")
        y2_done = sem("y2_done")
        y_arg = sem("y_arg")
        y_tanh = sem("y_tanh")
        fin = sem("fin")

        ssq_order = []
        for i, (kind, layer, *_rest) in enumerate(phases):
            if i == 0:
                ssq_order.append(("x", 0))
            if kind in ("conv_cv", "glu"):
                ssq_order.append(("mem", layer))
            if i in RESID:
                ssq_order.append(("x", RESID.index(i) + 1))

        def ssq_index(kind, n):
            return ssq_order.index((kind, n))

        block = ctx.enter_context(nc.Block())

        def groups(eng, n, body, peel_first=False, peel_last=False):
            a, b = int(peel_first), n - int(peel_last)
            if peel_first:
                body(0)
            if b - a == 1:
                body(a)
            elif b > a:
                with eng.Fori(a, b) as g:
                    body(g)
            if peel_last and n > 1:
                body(n - 1)

        last_phase = len(phases) - 1

        @block.sync
        def _(sp):
            w8_at = 0

            def load_x():
                for i in range(4):
                    sp.dma_start(X[:, 2 * i:2 * i + 2, :], x_in[:, 2 * i:2 * i + 2, :]).then_inc(x_in_done[i], 16)

            for kind, layer, u0, t0, c0, part in phases:
                if kind == "s5":
                    continue
                d0 = sum(1 for ph in phases if ph[0] == "down" and ph[2] < u0 and ph[5][1] == KF) * KD
                if kind == "down" and part == (0, KF):
                    def body(g):
                        for j in range(4):
                            for c, (a, b) in enumerate(CUTS):
                                i = 3 * j + c
                                sp.wait_ge(w_lo_done, u0 + 12 * g + i - SLOTS + 1)
                                sp.dma_start(raw[:, i % SLOTS, 0:(b - a) * P], wd[d0 + 4 * g + j, :, a * P:b * P])\
                                  .then_inc(raw_in[i % SLOTS], 16)
                    groups(sp, 2, body)
                elif kind == "down":
                    a, b = part

                    def body(g):
                        for i in range(4):
                            sp.wait_ge(w_lo_done, u0 + 4 * g + i - SLOTS + 1)
                            sp.dma_start(raw[:, i, 0:(b - a) * P], wd[d0 + 4 * g + i, :, a * P:b * P]).then_inc(raw_in[i], 16)
                    groups(sp, 2, body)
                else:
                    n = 2 * (part[1] - part[0]) if kind == "up" else {"conv_cv": 16, "glu": 16}.get(kind, 8)

                    def body(g):
                        for i in range(4):
                            if not (isinstance(g, int) and u0 + 4 * g + i < SLOTS):
                                sp.wait_ge(w_lo_done, u0 + 4 * g + i - SLOTS + 1)
                            sp.dma_start(raw[:, i, :], w8[w8_at + 4 * g + i]).then_inc(raw_in[i], 16)
                            if isinstance(g, int) and u0 + 4 * g + i == 0:
                                load_x()
                    groups(sp, n // 4, body, peel_first=(u0 == 0))
                    w8_at += n
            for k in range(KD):
                sp.wait_ge(fin, k + 1)
                sp.dma_start(out[:, k, :], X[:, k, :]).then_inc(out_done, 16)
            sp.wait_ge(out_done, 16 * KD)

        def by_step(ap):
            return ap.rearrange("p (n j) -> p j n", j=DT_T)

        def s5_halves(t):
            return t[:, :, :].rearrange("p (c q) n -> p c q n", c=2)

        def s5_rest(eng, c0, c):
            eng.tensor_tensor(by_step(m_lo[:, c, :]), a_buf[:, c % 2, :].rearrange("p (j n) -> p j n", j=DT_T),
                              by_step(m_hi[:, c, :]).bitcast(F32), ALU.subtract).then_inc(c_lo_done, 1)

        @block.gpsimd
        def _(pool):
            pool.dma_start(cols[:, :], cols_in).then_inc(cols_done, 16)
            pool.memset(ident[:, :], 0.0).then_inc(ident0, 1)
            pool.memset(ones[:, :], 1.0).then_inc(const_done, 1)
            pool.wait_ge(ident0, 1)
            pool.affine_select(out=ident[:, :], in_=ident[:, :], compare_op=ALU.not_equal, fill=1.0,
                               base=0, pattern=[[-1, P]], channel_multiplier=1).then_inc(const_done, 1)
            steps = [0]

            def squares(src, n, width, ready):
                def one(k):
                    ready(k)
                    pool.tensor_tensor(sq[:, 0:width], src(k), src(k), ALU.mult).then_inc(sq_done, 1)
                    pool.wait_ge(sq_done, steps[0] + 2 * k)
                    return pool.tensor_tensor(ssq[:, 0:width], ssq[:, 0:width], sq[:, 0:width], ALU.add)
                ready(0)
                pool.tensor_tensor(ssq[:, 0:width], src(0), src(0), ALU.mult).then_inc(sq_done, 1)
                pool.wait_ge(sq_done, steps[0] + 1)
                with pool.Fori(1, n - 1) as k:
                    one(k).then_inc(sq_done, 1)
                    pool.wait_ge(sq_done, steps[0] + 2 * k + 1)
                one(n - 1).then_inc(ssq_done, 1)
                steps[0] += 2 * n - 2

            def free_ssq(kind, n):
                if ssq_index(kind, n):
                    pool.wait_ge(sum_done, ssq_index(kind, n))

            M, A, S = ALU.mult, ALU.add, ALU.subtract
            count = [0]

            def step(ins):
                ins.then_inc(prep_step, 1)
                count[0] += 1
                pool.wait_ge(prep_step, count[0])

            def tt(o, a, b, op):
                step(pool.tensor_tensor(o, a, b, op))

            def ts(o, a, s1, s2, op0, op1=ALU.bypass):
                step(pool.tensor_scalar(o, a, s1, s2, op0, op1))

            def parameters():
                T = [tmp[:, j, :] for j in range(12)]
                pool.dma_start(pin[:, :, :], s5p).then_inc(s5p_done, 16)
                pool.dma_start(bcq[:, :, :], s5bc[0]).then_inc(bc_done, 16)
                pool.wait_ge(s5p_done, 16)
                are, aim, ldt = (pin[:, j, :] for j in range(3))
                lre, dt, th, mag, k, r, sn, cs, a, b, c, d = T

                def stt(o, a_, s_, b_, op0, op1):
                    ts(d, a_, s_, None, op0)
                    tt(o, d, b_, op1)

                def exp(o, x):
                    ts(x, x, 88.0, -87.0, ALU.min, ALU.max)
                    ts(k, x, 1.4426950408889634, MAGIC, M, A)
                    ts(k, k, -MAGIC, None, A)
                    stt(r, k, -0.693359375, x, M, A)
                    stt(r, k, 2.12194440e-4, r, M, A)
                    ts(o, r, 1.0 / 5040, None, M)
                    for f in (720, 120, 24, 6, 2, 1):
                        stt(o, o, 1.0 / f, r, A, M)
                    ts(o, o, 1.0, None, A)
                    ts(tmpi[:, :], k, 127.0, 8388608.0, A, M)
                    tt(o, o, tmpi[:, :].bitcast(F32), M)

                ts(lre, are, -1e-4, None, ALU.min)
                ts(a, ldt, 1.0, None, M)
                exp(dt, a)
                tt(th, aim, dt, M)
                tt(a, lre, dt, M)
                exp(mag, a)
                ts(k, th, 0.15915494309189535, MAGIC, M, A)
                ts(k, k, -MAGIC, None, A)
                for piece in TWO_PI:
                    stt(th, k, -piece, th, M, A)
                ts(r, th, 0.5, None, M)
                tt(a, r, r, M)
                sc = [(-1) ** j / math.factorial(2 * j + 1) for j in range(8)]
                cc = [(-1) ** j / math.factorial(2 * j) for j in range(9)]
                ts(sn, a, sc[7], None, M)
                for j in range(6, 0, -1):
                    stt(sn, sn, sc[j], a, A, M)
                stt(sn, sn, 1.0, r, A, M)
                ts(cs, a, cc[8], None, M)
                for j in range(7, 0, -1):
                    stt(cs, cs, cc[j], a, A, M)
                ts(cs, cs, 1.0, None, A)
                tt(b, sn, sn, M)
                stt(c, sn, 2.0, cs, M, M)
                ts(b, b, -2.0, 1.0, M, A)

                def cmul(o, x, y):
                    tt(k, x[0], y[0], M)
                    tt(r, x[1], y[1], M)
                    tt(o[0], k, r, S)
                    tt(k, x[0], y[1], M)
                    tt(r, x[1], y[0], M)
                    tt(o[1], k, r, A)

                pwr = [(pw[:, 0, j, :], pw[:, 1, j, :]) for j in range(5)]
                unr = [(un[:, 0, j, :], un[:, 1, j, :]) for j in range(7)]
                step(pool.memset(pwr[0][0], 1.0))
                step(pool.memset(pwr[0][1], 0.0))
                tt(pwr[1][0], mag, b, M)
                tt(pwr[1][1], mag, c, M)
                cmul(pwr[2], pwr[1], pwr[1])
                cmul(pwr[3], pwr[2], pwr[1])
                cmul(pwr[4], pwr[2], pwr[2])
                cmul((sn, cs), (b, c), (b, c))
                cmul(unr[0], (sn, cs), (sn, cs))
                for v in range(1, 7):
                    cmul(unr[v], unr[v - 1], unr[v - 1])
                tt(mag4[:, :], mag, mag, M)
                tt(mag4[:, :], mag4[:, :], mag4[:, :], M)
                tt(a, lre, lre, M)
                tt(b, aim, aim, M)
                pool.tensor_tensor(a, a, b, A).then_inc(den_done, 1)
                pool.wait_ge(rden_done, 1)
                ts(c, pwr[1][0], -1.0, None, A)
                tt(k, c, lre, M)
                tt(r, pwr[1][1], aim, M)
                tt(k, k, r, A)
                tt(coef[:, 0, :], k, b, M)
                tt(k, pwr[1][1], lre, M)
                tt(r, c, aim, M)
                tt(k, k, r, S)
                tt(coef[:, 1, :], k, b, M)

            def quarters(q0, q1):
                E, F, rot = cut_stage(stage[0])
                for q in range(q0, q1):
                    def op(o, a, b, f):
                        step(pool.tensor_tensor(o, a, b, f))

                    def cplx(o, x, y, t0, t1, neg_im=False):
                        op(t0, x[0], y[0], M)
                        op(t1, x[1], y[1], M)
                        op(o[0], t0, t1, S)
                        op(t0, x[0], y[1], M)
                        op(t1, x[1], y[0], M)
                        if neg_im:
                            step(pool.tensor_scalar(t0, t0, -1.0, None, M))
                        op(o[1], t0, t1, S if neg_im else A)

                    def tiles(ap):
                        return ap.rearrange("p (i f) -> p i f", i=QT)

                    def powers(dst, src, lo, hi, neg):
                        m = hi - lo
                        t = [w[:, 0:m * QT * 32].rearrange("p (k i f) -> p k i f", k=m, i=QT) for w in (w0, w1)]
                        p = [pw[:, j, lo:hi, QT * q:QT * (q + 1)][:, :, :, None].to_broadcast([P, m, QT, 32]) for j in range(2)]
                        cplx([dst[:, j, lo:hi, :, :] for j in range(2)], p,
                             [x[:, None, :, :].to_broadcast([P, m, QT, 32]) for x in src], *t, neg)

                    pool.wait_ge(bc_done, 16 * q + 16)
                    e0 = [E[:, j, 0, :, :] for j in range(2)]
                    cf = [coef[:, j, QT * q:QT * (q + 1)][:, :, None].to_broadcast([P, QT, 32]) for j in range(2)]
                    cplx(e0, cf, (tiles(bcq[:, 0, :]), tiles(bcq[:, 1, :])), tiles(w0[:, 0:QT * 32]), tiles(w1[:, 0:QT * 32]))
                    powers(E, e0, 1, 4, False)
                    step(pool.tensor_copy(F[:, 0, 0, :, :], tiles(bcq[:, 2, :])))
                    step(pool.tensor_scalar(F[:, 1, 0, :, :], tiles(bcq[:, 3, :]), -1.0, None, M))
                    powers(F, (tiles(bcq[:, 2, :]), tiles(bcq[:, 3, :])), 1, 5, True)
                    if q < 3:
                        pool.dma_start(bcq[:, :, :], s5bc[q + 1]).then_inc(bc_done, 16)
                    step(pool.memset(rot[:, 0, :, 0:1], 1.0))
                    step(pool.memset(rot[:, 1, :, 0:1], 0.0))
                    for v in range(7):
                        w = 1 << v
                        t = [x[:, 0:QT * w].rearrange("p (i n) -> p i n", i=QT) for x in (w0, w1)]
                        cplx([rot[:, j, :, w:2 * w] for j in range(2)],
                             [un[:, j, v, QT * q:QT * (q + 1)][:, :, None].to_broadcast([P, QT, w]) for j in range(2)],
                             [rot[:, j, :, 0:w] for j in range(2)], *t)
                    pool.dma_start(scratch[q], stage[0][:, :]).then_inc(spilled, 16)
                    pool.wait_ge(spilled, 16 * q + 16)

            e_size = 8 * QT * 32

            def load_e(q):
                pool.dma_start(stage[q % 2][:, 0:e_size], scratch[q][:, 0:e_size]).then_inc(e_in[q % 2], 16)

            def load_f(q):
                pool.dma_start(stage[q % 2][:, e_size:], scratch[q][:, e_size:]).then_inc(f_in[q % 2], 16)

            for landed in x_in_done[:(KD - VEC_SQ + 1) // 2]:
                pool.wait_ge(landed, 16)
            squares(lambda k: X[:, k, :], KD - VEC_SQ, SEQ, lambda k: None)
            for i, (kind, layer, u0, t0, c0, part) in enumerate(phases):
                if kind == "up" and part == CUTS[0]:
                    if layer == 0:
                        pool.wait_ge(unit_done, u0)
                        parameters()
                        quarters(0, 2)
                    else:
                        quarters(2, 4)
                        for q in range(2):
                            load_e(q)
                            load_f(q)
                if kind == "s5":
                    for r in range(4):
                        if r < 2:
                            pool.wait_ge(s5_lag, r + 1)
                            load_e(r + 2)
                        if r in (1, 2):
                            pool.wait_ge(s5_y, 2 * r)
                            load_f(r + 1)
                        cos, sin = (s5_halves(cut_stage(stage[r % 2])[2][:, j, :, :]) for j in range(2))
                        for ch in range(2):
                            z0, z2, co, si = (t[:, ch] for t in (s5_halves(r0), s5_halves(r2), cos, sin))
                            prod = nt_a[:, :].rearrange("p (q n) -> p q n", q=4)
                            pool.wait_ge(s5_scan, 8 * (2 * r + ch + 1))
                            if ch:
                                pool.tensor_tensor(prod, z0, si, M).then_inc(s5_prod, 1)
                                continue
                            if r:
                                pool.wait_ge(s5_im, 2 * r)
                            step(pool.tensor_tensor(prod, z0, si, M))
                            pool.wait_ge(s5_z0, 2 * r + ch + 1)
                            step(pool.tensor_tensor(z0, z2, co, M))
                            pool.tensor_tensor(z0, z0, prod, A).then_inc(s5_im, 1)
                            pool.wait_ge(s5_im, 2 * r + ch + 1)
                        if r:
                            for c in range(2 * r - 2, 2 * r):
                                pool.wait_ge(c_hi_done, c0 + c + 1)
                                s5_rest(pool, c0, c)
                if kind == "conv_cv":
                    pool.wait_ge(unit_done, u0)
                    pool.dma_start(mT[:, :, :], mem_in).then_inc(mem_done, 16)
                    free_ssq("mem", layer)
                    pool.wait_ge(mem_done, 16 * (layer + 1))
                    squares(lambda k: mT[:, k, :], KD, MEM, lambda k: None)
                if kind == "glu":
                    pool.wait_ge(c_lo_done, c0)
                    pool.dma_start(mT[:, :, :], mem_in).then_inc(mem_done, 16)
                    free_ssq("mem", layer)
                    pool.wait_ge(mem_done, 16 * (layer + 1))
                    squares(lambda k: mT[:, k, :], KD, MEM, lambda k: None)
                if i in RESID:
                    n = RESID.index(i) + 1
                    free_ssq("x", n)
                    if kind == "glu":
                        squares(lambda k: X[:, k, :], KD, SEQ, lambda k: pool.wait_ge(tile_done, t0 + 2 * k + 2))
                    else:
                        squares(lambda k: X[:, k, :], KD - (n in at_once), SEQ, lambda k: pool.wait_ge(tile_done, t0 + k + 1))

        LAG_BANK = 7

        def s5_bank(r, b):
            return (LAG_BANK, 5 if r == 1 else NORM_BANK)[b % 2]

        def s5_u4(copy, r, powers):
            for k in powers:
                for q in range(4):
                    ins = copy(u4[32 * k:32 * k + 32, q:QT:4, :], u_all[32 * q:32 * q + 32, 2 * r:2 * r + 2, DT_T - 1 - k, :])
            return ins

        def s5_et_copies(act, r, batches=range(4)):
            for b in batches:
                act.wait_ge(s5_tr, 4 * r + b + 1)
                act.activation(ET[:, r % 2, b // 2, 4 * (b % 2):4 * (b % 2) + 4, :], PS[:, s5_bank(r, b), :].rearrange("p (i s) -> p i s", i=4),
                               ACT.Copy).then_inc(s5_et, 1)

        def s5_lag_copies(act, r):
            act.wait_ge(s5_lag, r + 1)
            if r == 0:
                act.wait_ge(s5_mb0, 1)
            for ch in range(2):
                for q in range(4):
                    s = slice(32 * q, 32 * q + 32)
                    ins = act.activation(MB[s, ch, :, 32 * q:32 * q + 32],
                                         PS[s, LAG_BANK, ch * P:(ch + 1) * P].rearrange("p (l f) -> p l f", l=4), ACT.Copy)
            ins.then_inc(s5_mb, 1)

        @block.scalar
        def _(act):
            def split(u, slot):
                if not isinstance(u, int) or u >= SLOTS:
                    act.wait_ge(unit_done, u - SLOTS + 1)
                    act.wait_ge(raw_in[slot], 4 * (u - slot) + 16)
                else:
                    act.wait_ge(raw_in[slot], 16)
                act.activation(w_hi[:, slot, :], raw[:, slot, :], ACT.Copy).then_inc(w_hi_done, 1)

            def ahead(u, i):
                if isinstance(u, int) and u + LEAD >= UNITS:
                    return
                split(u + LEAD, (i + LEAD) % SLOTS)

            def chunk_hi(c, par, dst):
                act.wait_ge(c_ready, c + 1)
                act.activation(dst, a_buf[:, par, :], ACT.Copy).then_inc(c_hi_done, 1)

            def h_split(n, k):
                g = gain_col(n)
                act.activation(h_hi[:, k, :], X[:, k, :], ACT.Copy, scale=cols[:, bass.ds(g + k, 1)]).then_inc(h_hi_done, 1)

            split(0, 0)
            act.wait_ge(cols_done, 16)
            for k in range(KD):
                act.wait_ge(x_in_done[k // 2], 16)
                h_split(0, k)
            for u in range(1, LEAD):
                split(u, u)

            g_count = 0
            n_mem = 0
            kv = 0
            heads = 0
            for i_ph, (kind, layer, u0, t0, c0, part) in enumerate(phases):
                peel = i_ph == last_phase

                def mem_hi():
                    act.wait_ge(n_lo_done, n_mem * (KD + 1) + 1)
                    for k in range(KD):
                        act.activation(n_hi[:, k, :], mT[:, k, :], ACT.Copy,
                                       scale=cols[:, (layer * 5 + 3) * KD + k:(layer * 5 + 3) * KD + k + 1])\
                           .then_inc(n_hi_done, 1)

                if kind == "up":
                    def body(g):
                        for i in range(4):
                            ahead(u0 + 4 * g + i, i)
                            if i % 2:
                                p = 2 * g + i // 2
                                act.wait_ge(g_done, g_count + p + 1)
                                act.activation(t_buf[:, i // 2, :], g_buf[:, i // 2, :], ACT.Tanh, scale=0.5)\
                                   .then_inc(tanh_done, 1)
                                chunk_hi(c0 + p, i // 2, dst[:, p, :])
                    dst = f_hi if part == (0, KF) else m_hi
                    groups(act, (part[1] - part[0]) // 2, body, peel_first=(u0 == 0))
                    g_count += part[1] - part[0]
                elif kind == "down":
                    n = RESID.index(i_ph) + 1 if i_ph in RESID else None
                    per = 3 if part == (0, KF) else 1
                    if phases[i_ph + 1:] and phases[i_ph + 1][0] == "s5":
                        s5_et_copies(act, 0)
                        s5_lag_copies(act, 0)

                    def body(g):
                        for i in range(4 * per):
                            ahead(u0 + 4 * per * g + i, i)
                            if i % per == per - 1 and n in h_base:
                                k = 4 * g + i // per
                                act.wait_ge(tile_done, t0 + k + 1)
                                h_split(n, k)
                    groups(act, 2, body, peel_last=peel)
                elif kind == "conv_cv":
                    def body(g):
                        for i in range(4):
                            ahead(u0 + 4 * g + i, i)
                    groups(act, 4, body)
                    g_count += KD
                elif kind in ("conv_b", "q"):
                    def body(g):
                        for i in range(4):
                            ahead(u0 + 4 * g + i, i)
                            chunk_hi(c0 + 4 * g + i, i % 2, m_hi[:, 4 * g + i, :])
                    groups(act, 2, body)
                elif kind in ("conv_o", "o"):
                    n = RESID.index(i_ph) + 1

                    def body(g):
                        for i in range(4):
                            ahead(u0 + 4 * g + i, i)
                            k = 4 * g + i
                            act.wait_ge(tile_done, t0 + k + 1)
                            h_split(n, k)
                    if kind == "conv_o":
                        mem_hi()
                        n_mem += 1
                    groups(act, 2, body)
                elif kind == "glu":
                    n = RESID.index(i_ph) + 1

                    def body(g):
                        if isinstance(g, int):
                            mem_hi()
                        for i in range(4):
                            ahead(u0 + 4 * g + i, i)
                            if i % 2:
                                act.wait_ge(unit_done, u0 + 4 * g + i + 1)
                                act.activation(t_buf[:, i // 2, :], PS[:, i, :], ACT.Tanh, scale=0.25)\
                                   .then_inc(tanh_done, 1)
                                k = 2 * g + i // 2
                                act.wait_ge(tile_done, t0 + 2 * k + 2)
                                h_split(n, k)
                    groups(act, 4, body, peel_last=True)
                    n_mem += 1
                elif kind == "k":
                    def body(g):
                        for i in range(4):
                            ahead(u0 + 4 * g + i, i)
                            act.wait_ge(unit_done, u0 + 4 * g + i + 1)
                            act.activation(k_hi[:, 4 * g + i, :], PS[:, i, 0:MEM], ACT.Copy).then_inc(kv_hi_done, 1)
                    groups(act, 2, body)
                elif kind == "core":
                    def v(g):
                        act.wait_ge(unit_done, u0 + 4 * g + 4)
                        for mc in range(2):
                            act.activation(v_hi[:, mc, g * 512:(g + 1) * 512], PS[:, 4 + 2 * g + mc, :], ACT.Copy)\
                               .then_inc(kv_hi_done, 1)

                    def exp(h):
                        act.wait_ge(bias_done, heads + h + 1)
                        for t in range(4):
                            ins = act.activation(prob[:, h % 2, t, :], PS[:, 2 * (h % 2) + t // 2, (t % 2) * MEM:(t % 2 + 1) * MEM],
                                                 ACT.Exp, bias=nb[:, h % 2, t:t + 1], scale=1.0 / 16,
                                                 accum_out=esum[:, h % 2, t:t + 1])
                        ins.then_inc(exp_done, 1)

                    def pt(h):
                        act.wait_ge(pt_done, heads + h + 1)
                        if h or heads:
                            act.wait_ge(pv_done, heads + h)
                        act.activation(pt_hi[:, :, :], PS[:, 4:6, :], ACT.Copy).then_inc(pt_hi_done, 1)

                    def o(h):
                        act.wait_ge(pv_done, heads + h + 1)
                        act.activation(m_hi[:, 2 * h:2 * h + 2, :], PS[:, 6:8, :], ACT.Copy).then_inc(o_hi_done, 1)

                    for i in range(4):
                        ahead(u0 + i, i)
                    v(0)
                    ahead(u0 + 4, 0)
                    exp(0)
                    exp(1)
                    for i in range(1, 4):
                        ahead(u0 + 4 + i, i)
                    v(1)
                    for h in range(HEADS):
                        pt(h)
                        if h + 2 < HEADS:
                            exp(h + 2)
                        o(h)
                    heads += HEADS
                elif kind == "s5":
                    def copy(o, a):
                        return act.activation(o, a, ACT.Copy)

                    def square(r):
                        for ch in range(2):
                            act.wait_ge(y_done, 2 * r + ch + 1)
                            act.activation(t_buf[:, ch, :], g_buf[:, ch, :], ACT.Square, scale=math.sqrt(0.044715)).then_inc(y2_done, 1)

                    def tanh(r):
                        for ch in range(2):
                            act.wait_ge(y_arg, 2 * r + ch + 1)
                            act.activation(t_buf[:, ch, :], a_buf[:, ch, :], ACT.Tanh, scale=math.sqrt(2 / math.pi)).then_inc(y_tanh, 1)

                    def hi(r):
                        for ch in range(2):
                            c = 2 * r + ch
                            act.wait_ge(c_ready, c0 + c + 1)
                            act.activation(by_step(m_hi[:, c, :]), a_buf[:, ch, :].rearrange("p (j n) -> p j n", j=DT_T), ACT.Copy)\
                               .then_inc(c_hi_done, 1)

                    def u4_of(r):
                        act.wait_ge(s5_u, 2 * r + 2)
                        act.wait_ge(s5_x, r)
                        s5_u4(copy, r, range(4)).then_inc(s5_u4a, 1)

                    s5_et_copies(act, 1, range(0, 2))
                    act.wait_ge(s5_u, 2)
                    s5_u4(copy, 0, (0, 1)).then_inc(s5_u4a, 1)
                    s5_et_copies(act, 1, range(2, 4))
                    u4_of(1)
                    s5_et_copies(act, 2)
                    u4_of(2)
                    s5_lag_copies(act, 1)
                    for r in range(1, 4):
                        square(r - 1)
                        tanh(r - 1)
                        if r == 1:
                            s5_et_copies(act, 3)
                            u4_of(3)
                        if r < 3:
                            s5_lag_copies(act, r + 1)
                        hi(r - 1)
                    square(3)
                    tanh(3)
                    hi(3)

        def s5_vector(dve, i_ph, c0, norm):
            M, A, S = ALU.mult, ALU.add, ALU.subtract
            count = [0]

            def op(o, a, b, f):
                dve.tensor_tensor(o, a, b, f).then_inc(s5_step, 1)
                count[0] += 1

            def through():
                dve.wait_ge(s5_step, count[0])

            def u_of(r):
                for ch in range(2):
                    k = 2 * r + ch
                    g = gain_col(norm_of(i_ph)) + k
                    dve.scalar_tensor_tensor(u_all[:, k, :, :], by_step(X[:, k, :]), cols[:, g:g + 1],
                                             by_step(rstd[:, :]), M, M).then_inc(s5_u, 1)

            def gelu_arg(r):
                for ch in range(2):
                    c = 2 * r + ch
                    dve.wait_ge(y2_done, c + 1)
                    if r:
                        dve.wait_ge(c_lo_done, c0 + c - 1)
                    dve.scalar_tensor_tensor(a_buf[:, ch, :], t_buf[:, ch, :], 1.0, g_buf[:, ch, :], A, M).then_inc(y_arg, 1)

            def gelu(r):
                for ch in range(2):
                    dve.wait_ge(y_tanh, 2 * r + ch + 1)
                    dve.scalar_tensor_tensor(a_buf[:, ch, :], t_buf[:, ch, :], 1.0, g_buf[:, ch, :], A, M).then_inc(c_ready, 1)

            def outputs(r):
                if r:
                    dve.wait_ge(c_ready, c0 + 2 * r)
                for ch in range(2):
                    c = 2 * r + ch
                    dve.wait_ge(s5_y, c + 1)
                    dve.scalar_tensor_tensor(g_buf[:, ch, :], u_all[:, c, :, :].rearrange("p j n -> p (j n)"),
                                             cols[:, G_SKIP + c:G_SKIP + c + 1], PS[:, 5 + ch, :], M, A).then_inc(y_done, 1)

            norm("x", norm_of(i_ph), SEQ)
            u_of(0)
            dve.wait_ge(s5_u, 2)
            s5_u4(dve.tensor_copy, 0, (2, 3)).then_inc(s5_u4v, 1)
            for r in range(1, 4):
                u_of(r)
            px = [PS[:, 0:4, :].rearrange("p q (c r n) -> p r c q n", c=2, r=2)[:, j] for j in range(2)]
            R = [s5_halves(t) for t in (r0, r1, r2, r3)]
            for r in range(4):
                rot = cut_stage(stage[r % 2])[2]
                cos, sin = (s5_halves(rot[:, j, :, :]) for j in range(2))
                dve.wait_ge(f_in[r % 2], 16 * (r // 2 + 1))
                dve.wait_ge(s5_x, r + 1)
                if r:
                    dve.wait_ge(s5_im, 2 * r)
                    dve.wait_ge(s5_re, 2 * r)
                op(R[2], px[1], cos, M)
                op(R[3], px[0], sin, M)
                through()
                op(R[2], R[2], R[3], S)
                if r:
                    outputs(r - 1)
                op(R[0], px[0], cos, M)
                op(R[1], px[1], sin, M)
                through()
                dve.tensor_tensor(R[0], R[0], R[1], A).then_inc(s5_xfree, 1)
                dve.wait_ge(s5_xfree, r + 1)
                if r:
                    gelu_arg(r - 1)
                for ch in range(2):
                    for i in range(4 * ch, 4 * ch + 4):
                        for t in (r0, r2):
                            dve.tensor_tensor_scan(t[:, i, :], mag4[:, QT * r + i:QT * r + i + 1].to_broadcast([P, NCH]),
                                                   t[:, i, :], 0.0, M, A).then_inc(s5_scan, 1)
                    dve.wait_ge(s5_scan, 8 * (2 * r + ch + 1))
                    z0, z1, z2, z3, co, si = (t[:, ch] for t in R + [cos, sin])
                    dve.tensor_tensor(z1, z0, co, M).then_inc(s5_z0, 1)
                    op(z3, z2, si, M)
                    through()
                    dve.wait_ge(s5_z0, 2 * r + ch + 1)
                    dve.tensor_tensor(z1, z1, z3, S).then_inc(s5_re, 1)
                prod = nt_a[:, :].rearrange("p (q n) -> p q n", q=4)
                dve.wait_ge(s5_prod, r + 1)
                op(z0, z2, co, M)
                through()
                dve.tensor_tensor(z0, z0, prod, A).then_inc(s5_im, 1)
                if r:
                    gelu(r - 1)
            outputs(3)
            gelu_arg(3)
            gelu(3)
            for c in range(6, 8):
                dve.wait_ge(c_hi_done, c0 + c + 1)
                dve.wait_ge(c_lo_done, c0 + c)
                s5_rest(dve, c0, c)

        @block.vector
        def _(dve):
            def split(u, slot):
                dve.wait_ge(w_hi_done, u + 1)
                dve.tensor_tensor(w_lo[:, slot, :], raw[:, slot, :], w_hi[:, slot, :].bitcast(F32), ALU.subtract)\
                   .then_inc(w_lo_done, 1)

            def ahead(u, i):
                if isinstance(u, int) and u + LEAD >= UNITS:
                    return
                split(u + LEAD, (i + LEAD) % SLOTS)

            def chunk_lo(c, par, dst, hi):
                dve.wait_ge(c_hi_done, c + 1)
                dve.tensor_tensor(dst, a_buf[:, par, :], hi.bitcast(F32), ALU.subtract).then_inc(c_lo_done, 1)

            def h_rest(n, k):
                dve.wait_ge(h_hi_done, h_base[n] + k + 1)
                dve.scalar_tensor_tensor(h_lo[:, k, :], X[:, k, :], cols[:, bass.ds(gain_col(n) + k, 1)],
                                         h_hi[:, k, :].bitcast(F32), ALU.mult, ALU.subtract).then_inc(h_lo_done, 1)

            nsteps = [0]

            def norm(kind, n, width):
                def step(ins):
                    ins.then_inc(newton, 1)
                    nsteps[0] += 1
                    dve.wait_ge(newton, nsteps[0])
                if kind == "x":
                    a, y, t = (small[:, j, :] for j in range(3))
                    sums = PS[:, NORM_BANK, 0:SEQ // P]
                else:
                    a, y, t = nt_a[:, 0:width], rstd[:, 0:width], u_buf[:, 0:width]
                    sums = PS[:, NORM_BANK, 0:width]
                dve.wait_ge(sum_done, ssq_index(kind, n) + 1)
                step(dve.tensor_scalar(a, sums, 1.0 / D, EPS, ALU.mult, ALU.add))
                step(dve.tensor_scalar(y.bitcast(I32), a.bitcast(I32), -0.5, float(0x5f3759df), ALU.mult, ALU.add))
                for _ in range(3):
                    step(dve.tensor_tensor(t, y, y, ALU.mult))
                    step(dve.scalar_tensor_tensor(t, t, -0.5, a, ALU.mult, ALU.mult))
                    step(dve.scalar_tensor_tensor(y, t, 1.5, y, ALU.add, ALU.mult))
                if kind == "x":
                    dve.tensor_tensor(nt_a[:, :].rearrange("p (t j) -> p t j", j=P), ident[:, None, :].to_broadcast([P, SEQ // P, P]),
                                      y[:, :, None].to_broadcast([P, SEQ // P, P]), ALU.mult).then_inc(diag_done, 1)
                    dve.wait_ge(spread_done, n + 1)
                    step(dve.tensor_copy(rstd[:, :], PS[:, NORM_BANK, :]))

            def mem_rest(layer, n_mem):
                norm("mem", layer, MEM)
                dve.tensor_tensor(mT[:, :, :], mT[:, :, :], rstd[:, None, 0:MEM].to_broadcast([P, KD, MEM]), ALU.mult)\
                   .then_inc(n_lo_done, 1)
                dve.wait_ge(n_lo_done, n_mem * (KD + 1) + 1)
                for k in range(KD):
                    dve.wait_ge(n_hi_done, n_mem * KD + k + 1)
                    g = (layer * 5 + 3) * KD + k
                    dve.scalar_tensor_tensor(n_lo[:, k, :], mT[:, k, :], cols[:, g:g + 1], n_hi[:, k, :].bitcast(F32),
                                             ALU.mult, ALU.subtract).then_inc(n_lo_done, 1)

            split(0, 0)
            dve.wait_ge(cols_done, 16)
            for k in range(KD):
                dve.wait_ge(x_in_done[k // 2], 16)
                h_rest(0, k)
            for u in range(1, LEAD):
                split(u, u)
            part_sum, product = g_buf[:, 0, :], g_buf[:, 1, :]
            dve.tensor_tensor(part_sum, X[:, KD - VEC_SQ, :], X[:, KD - VEC_SQ, :], ALU.mult).then_inc(sq0_done, 1)
            for j in range(1, VEC_SQ):
                k = KD - VEC_SQ + j
                dve.tensor_tensor(product, X[:, k, :], X[:, k, :], ALU.mult).then_inc(sq0_done, 1)
                dve.wait_ge(sq0_done, 2 * j)
                dve.tensor_tensor(part_sum, part_sum, product, ALU.add).then_inc(sq0_done, 1)
                dve.wait_ge(sq0_done, 2 * j + 1)

            pairs = 0
            g_count = 0
            u_count = 0
            n_mem = 0
            kv = 0
            heads = 0
            for i_ph, (kind, layer, u0, t0, c0, part) in enumerate(phases):
                peel = i_ph == last_phase
                if kind == "up":
                    def body(g):
                        first = isinstance(g, int) and g == 0 and part[0] == 0
                        for i in range(4):
                            p = 2 * g + i // 2
                            b = i // 2
                            ahead(u0 + 4 * g + i, i)
                            if first and i == 0:
                                norm("x", norm_of(i_ph), SEQ)
                            dve.wait_ge(unit_done, u0 + 4 * g + i + 1)
                            if i % 2 == 0:
                                dve.tensor_tensor(g_buf[:, b, :], PS[:, i, :], rstd[:, :], ALU.mult).then_inc(g_done, 1)
                                dve.wait_ge(g_done, g_count + p + 1)
                                continue
                            dve.tensor_tensor(u_buf[:, :], PS[:, i, :], rstd[:, :], ALU.mult).then_inc(tile_done, 2)
                            dve.wait_ge(tile_done, t0 + 2 * p + 2)
                            dve.tensor_tensor(u_buf[:, :], u_buf[:, :], g_buf[:, b, :], ALU.mult).then_inc(u_done, 1)
                            dve.wait_ge(u_done, u_count + p + 1)
                            dve.wait_ge(tanh_done, pairs + p + 1)
                            dve.scalar_tensor_tensor(a_buf[:, b, :], t_buf[:, b, :], 1.0, u_buf[:, :], ALU.add, ALU.mult)\
                               .then_inc(c_ready, 1)
                            chunk_lo(c0 + p, b, lo[:, p, :], hi[:, p, :])
                    hi, lo = (f_hi, f_lo) if part == (0, KF) else (m_hi, m_lo)
                    n = part[1] - part[0]
                    groups(dve, n // 2, body, peel_first=(part[0] == 0))
                    pairs += n
                    g_count += n
                    u_count += n
                    if part == CUTS[0] and layer == 0:
                        dve.wait_ge(den_done, 1)
                        dve.reciprocal(tmp[:, 9, :], tmp[:, 8, :]).then_inc(rden_done, 1)
                elif kind == "down":
                    n = RESID.index(i_ph) + 1 if i_ph in RESID else None
                    per = 3 if part == (0, KF) else 1
                    if phases[i_ph + 1:] and phases[i_ph + 1][0] == "s5":
                        dve.memset(MB[:, :, :, :], 0.0).then_inc(s5_mb0, 1)

                    def body(g):
                        for i in range(4 * per):
                            ahead(u0 + 4 * per * g + i, i)
                            if i % per == per - 1:
                                k = 4 * g + i // per
                                dve.wait_ge(unit_done, u0 + 4 * per * g + i + 1)
                                dve.scalar_tensor_tensor(X[:, k, :], PS[:, i // per, :], 0.25, X[:, k, :], ALU.mult, ALU.add)\
                                   .then_inc(tile_done, 1)
                                if n in h_base:
                                    h_rest(n, k)
                    groups(dve, 2, body, peel_last=peel)
                    if n in at_once:
                        dve.wait_ge(tile_done, t0 + KD)
                        dve.tensor_tensor(g_buf[:, 1, :], X[:, KD - 1, :], X[:, KD - 1, :], ALU.mult).then_inc(sq_last_done, 1)
                elif kind == "conv_cv":
                    dve.memset(cu[:, :, 0:2], 0.0).then_inc(conv_step, 1)

                    def body(g):
                        first = isinstance(g, int) and g == 0
                        for i in range(4):
                            b = i // 2
                            ahead(u0 + 4 * g + i, i)
                            if first and i == 0:
                                norm("x", norm_of(i_ph), SEQ)
                            dve.wait_ge(unit_done, u0 + 4 * g + i + 1)
                            k = 2 * g + b
                            if i % 2 == 0:
                                dve.tensor_tensor(g_buf[:, b, :], PS[:, i, :], rstd[:, :], ALU.mult).then_inc(g_done, 1)
                                dve.wait_ge(g_done, g_count + k + 1)
                                continue
                            dve.tensor_tensor(u_buf[:, :], PS[:, i, :], rstd[:, :], ALU.mult).then_inc(tile_done, 2)
                            dve.wait_ge(tile_done, t0 + 2 * k + 2)
                            dve.tensor_tensor(cu[:, k, 2:2 + SEQ], u_buf[:, :], g_buf[:, b, :], ALU.mult).then_inc(u_done, 1)
                            dve.wait_ge(u_done, u_count + 2 * k + 1)
                            dve.wait_ge(conv_step, 1 + 2 * k)
                            col = G_CONV + k
                            dve.tensor_scalar(cv[:, k, :], cu[:, k, 0:SEQ], cols[:, bass.ds(col, 1)], None, ALU.mult)\
                               .then_inc(conv_step, 1)
                            dve.wait_ge(conv_step, 2 + 2 * k)
                            dve.scalar_tensor_tensor(cv[:, k, :], cu[:, k, 1:1 + SEQ], cols[:, bass.ds(col + KD, 1)],
                                                     cv[:, k, :], ALU.mult, ALU.add).then_inc(conv_step, 1)
                            dve.wait_ge(conv_step, 3 + 2 * k)
                            dve.scalar_tensor_tensor(cv[:, k, :], cu[:, k, 2:2 + SEQ], cols[:, bass.ds(col + 2 * KD, 1)],
                                                     cv[:, k, :], ALU.mult, ALU.add).then_inc(u_done, 1)
                            dve.wait_ge(u_done, u_count + 2 * k + 2)
                    groups(dve, 4, body, peel_first=True)
                    g_count += KD
                    u_count += 2 * KD
                elif kind in ("conv_b", "q"):
                    def body(g):
                        first = isinstance(g, int) and g == 0
                        for i in range(4):
                            k = 4 * g + i
                            ahead(u0 + 4 * g + i, i)
                            dve.wait_ge(unit_done, u0 + 4 * g + i + 1)
                            if kind == "q":
                                dve.tensor_tensor(a_buf[:, i % 2, :], PS[:, i, :], rstd[:, :], ALU.mult).then_inc(tile_done, 1)
                                dve.wait_ge(tile_done, t0 + k + 1)
                                dve.sem_inc(c_ready, 1)
                            else:
                                dve.tensor_tensor(u_buf[:, :], PS[:, i, :], rstd[:, :], ALU.mult).then_inc(tile_done, 1)
                                dve.wait_ge(tile_done, t0 + k + 1)
                                dve.tensor_tensor(a_buf[:, i % 2, :], u_buf[:, :], cv[:, k, :], ALU.mult).then_inc(c_ready, 1)
                            chunk_lo(c0 + k, i % 2, m_lo[:, k, :], m_hi[:, k, :])
                    groups(dve, 2, body)
                elif kind in ("conv_o", "o"):
                    n = RESID.index(i_ph) + 1

                    def body(g):
                        for i in range(4):
                            k = 4 * g + i
                            ahead(u0 + 4 * g + i, i)
                            dve.wait_ge(unit_done, u0 + 4 * g + i + 1)
                            dve.tensor_tensor(X[:, k, :], PS[:, i, :], X[:, k, :], ALU.add).then_inc(tile_done, 1)
                            h_rest(n, k)
                    if kind == "conv_o":
                        mem_rest(layer, n_mem)
                        n_mem += 1
                    groups(dve, 2, body)
                elif kind == "glu":
                    n = RESID.index(i_ph) + 1

                    def body(g):
                        if isinstance(g, int):
                            mem_rest(layer, n_mem)
                        for i in range(4):
                            ahead(u0 + 4 * g + i, i)
                            if i % 2:
                                k = 2 * g + i // 2
                                b = i // 2
                                dve.wait_ge(unit_done, u0 + 4 * g + i + 1)
                                dve.wait_ge(tanh_done, pairs + k + 1)
                                dve.scalar_tensor_tensor(u_buf[:, :], t_buf[:, b, :], 1.0, PS[:, i - 1, :], ALU.add, ALU.mult)\
                                   .then_inc(u_done, 1)
                                dve.wait_ge(u_done, u_count + k + 1)
                                dve.scalar_tensor_tensor(X[:, k, :], u_buf[:, :], 0.25, X[:, k, :], ALU.mult, ALU.add)\
                                   .then_inc(tile_done, 2)
                                h_rest(n, k)
                    groups(dve, 4, body, peel_last=True)
                    n_mem += 1
                    pairs += KD
                    u_count += KD
                elif kind == "k":
                    def body(g):
                        first = isinstance(g, int) and g == 0
                        for i in range(4):
                            k = 4 * g + i
                            ahead(u0 + 4 * g + i, i)
                            if first and i == 2:
                                norm("x", norm_of(i_ph), SEQ)
                            dve.wait_ge(kv_hi_done, kv + k + 1)
                            dve.tensor_tensor(k_lo[:, k, :], PS[:, i, 0:MEM], k_hi[:, k, :].bitcast(F32), ALU.subtract)\
                               .then_inc(tile_done, 1)
                    groups(dve, 2, body, peel_first=True)
                    kv += KD
                elif kind == "core":
                    def v(g):
                        for mc in range(2):
                            dve.wait_ge(kv_hi_done, kv + 2 * g + mc + 1)
                            s = slice(g * 512, (g + 1) * 512)
                            dve.tensor_tensor(v_lo[:, mc, s], PS[:, 4 + 2 * g + mc, :], v_hi[:, mc, s].bitcast(F32), ALU.subtract)\
                               .then_inc(tile_done, 1)

                    def bias(h):
                        dve.wait_ge(score_done, heads + h + 1)
                        b = 2 * (h % 2)
                        dve.tensor_reduce(mx[:, h % 2, :], PS[:, b:b + 2, :].rearrange("p b (t m) -> p (b t) m", t=2), AX.X, ALU.max)\
                           .then_inc(att_step, 1)
                        att_n[0] += 1
                        dve.wait_ge(att_step, att_n[0])
                        dve.tensor_scalar(nb[:, h % 2, :], mx[:, h % 2, :], -1.0 / 16, None, ALU.mult).then_inc(bias_done, 1)

                    def normalise(h):
                        dve.wait_ge(exp_done, heads + h + 1)
                        dve.reciprocal(rsum[:, h % 2, :], esum[:, h % 2, :]).then_inc(att_step, 1)
                        att_n[0] += 1
                        dve.wait_ge(att_step, att_n[0])
                        for t in range(4):
                            ins = dve.tensor_scalar(prob[:, h % 2, t, :], prob[:, h % 2, t, :], rsum[:, h % 2, t:t + 1], None, ALU.mult)
                        ins.then_inc(prob_done, 1)

                    def pt(h):
                        dve.wait_ge(pt_hi_done, heads + h + 1)
                        dve.tensor_tensor(pt_lo[:, :, :], PS[:, 4:6, :], pt_hi[:, :, :].bitcast(F32), ALU.subtract).then_inc(pt_lo_done, 1)

                    def o(h):
                        dve.wait_ge(o_hi_done, heads + h + 1)
                        s = slice(2 * h, 2 * h + 2)
                        dve.tensor_tensor(m_lo[:, s, :], PS[:, 6:8, :], m_hi[:, s, :].bitcast(F32), ALU.subtract).then_inc(o_lo_done, 1)

                    att_n = [2 * heads]
                    for i in range(4):
                        ahead(u0 + i, i)
                    v(0)
                    ahead(u0 + 4, 0)
                    bias(0)
                    bias(1)
                    normalise(0)
                    ahead(u0 + 5, 1)
                    normalise(1)
                    ahead(u0 + 6, 2)
                    ahead(u0 + 7, 3)
                    v(1)
                    kv += 4
                    for h in range(HEADS):
                        pt(h)
                        if 2 <= h + 1 < HEADS:
                            normalise(h + 1)
                        if h + 2 < HEADS:
                            bias(h + 2)
                        o(h)
                    heads += HEADS
                elif kind == "s5":
                    s5_vector(dve, i_ph, c0, norm)
            norm("x", len(RESID), SEQ)
            for k in range(KD):
                dve.scalar_tensor_tensor(X[:, k, :], X[:, k, :], cols[:, G_FINAL + k:G_FINAL + k + 1], rstd[:, :], ALU.mult, ALU.mult)\
                   .then_inc(fin, 1)

        def s5_turn(te, r, batches=range(4)):
            E = cut_stage(stage[r % 2])[0]
            te.wait_ge(e_in[r % 2], 16 * (r // 2 + 1))
            if r:
                te.wait_ge(s5_mb, max(1, r - 1))
                te.wait_ge(s5_et, 4 * r)
            if r > 1:
                te.wait_ge(s5_u, 2)
            for b in batches:
                if b >= 2:
                    te.wait_ge(s5_et, 4 * r + b - 1)
                for j in range(4):
                    i = 4 * (b % 2) + j
                    mm = te.transpose(PS[:, s5_bank(r, b), j * P:(j + 1) * P], E[:, b // 2, :, i, :], ident[:, :])
                mm.then_inc(s5_tr, 1)

        def s5_lags(te, r):
            E, F, _ = cut_stage(stage[r % 2])
            te.wait_ge(f_in[r % 2], 16 * (r // 2 + 1))
            te.wait_ge(s5_et, 4 * (min(r + 1, 3) if r else 0) + 3)
            for ch in range(2):
                for part, start in ((0, True), (1, False)):
                    for q in range(4):
                        i = 4 * ch + q
                        mm = te.matmul(PS[32 * q:32 * q + 32, LAG_BANK, ch * P:(ch + 1) * P], E[:, part, 0, i, :],
                                       F[:, part, 0:4, i, :], start=start, stop=not start, skip_group_check=True)
            mm.then_inc(s5_lag, 1)

        def s5_inputs(te, r):
            te.wait_ge(s5_et, 4 * r + 4)
            te.wait_ge(s5_u4a, r + 1)
            if r == 0:
                te.wait_ge(s5_u4v, 1)
            for i in range(QT):
                for ri in range(2):
                    c = 2 * (i // 4) + ri
                    mm = te.matmul(PS[:, i % 4, c * P:(c + 1) * P], ET[:, r % 2, ri, i, :], u4[:, i, :], start=True, stop=True,
                                   skip_group_check=True)
            mm.then_inc(s5_x, 1)

        def s5_within(te, r):
            te.wait_ge(s5_mb, r + 1)
            if r == 0:
                te.wait_ge(s5_et, 8)
            te.wait_ge(s5_u, 2 * r + 2)
            if r:
                te.wait_ge(y_done, 2 * r)
            for ch in range(2):
                for l in range(DT_T):
                    te.matmul(PS[:, 5 + ch, l * NCH:], MB[:, ch, l, :], u_all[:, 2 * r + ch, 0:DT_T - l, :], start=l == 0, stop=False,
                              skip_group_check=True)

        def s5_outputs(te, r):
            F = cut_stage(stage[r % 2])[1]
            for ch in range(2):
                te.wait_ge(s5_re, 2 * r + ch + 1)
                te.wait_ge(s5_im, 2 * r + ch + 1)
                for j in range(DT_T):
                    for ri, state in ((0, r1), (1, r0)):
                        for q in range(4):
                            i = 4 * ch + q
                            mm = te.matmul(PS[32 * q:32 * q + 32, 5 + ch, j * NCH + 1:(j + 1) * NCH], F[:, ri, j + 1, i, :],
                                           state[:, i, 0:NCH - 1], start=False, stop=ri == 1 and j == DT_T - 1, skip_group_check=True)
                mm.then_inc(s5_y, 1)

        @block.tensor
        def _(te):
            def three(ps, whi, wlo, xhi, xlo, start, stop):
                te.matmul(ps, whi, xhi, start=start, stop=False)
                te.matmul(ps, whi, xlo, start=False, stop=False)
                return te.matmul(ps, wlo, xhi, start=False, stop=stop)

            def unit(u, slot, bank, ks, xh, xl, start, stop, ready=None, width=SEQ):
                te.wait_ge(w_lo_done, u + 1)
                for t, k in enumerate(ks):
                    if ready:
                        ready(k)
                    s = slice(t * P, (t + 1) * P)
                    mm = three(PS[:, bank, 0:width], w_hi[:, slot, s], w_lo[:, slot, s], xh[:, k, :], xl[:, k, :],
                               start and t == 0, stop and t == len(ks) - 1)
                mm.then_inc(unit_done, 1)

            def bank_free(t):
                if not (isinstance(t, int) and t < 4):
                    te.wait_ge(tile_done, t - 3)

            def sums(kind, n, width):
                te.wait_ge(ssq_done, ssq_index(kind, n) + 1)
                if ssq_index(kind, n) == 0:
                    te.wait_ge(const_done, 2)
                if kind == "x":
                    parts = [ssq] + [g_buf[:, 0, :]] * (n == 0) + [g_buf[:, 1, :]] * (n in at_once)
                    if n in at_once:
                        te.wait_ge(sq_last_done, at_once.index(n) + 1)
                    if n == 0:
                        te.wait_ge(sq0_done, 2 * VEC_SQ - 1)
                    for t in range(SEQ // P):
                        for part_sum in parts:
                            mm = te.matmul(PS[:, NORM_BANK, t:t + 1], part_sum[:, t * P:(t + 1) * P], ones[:, 0:1],
                                           start=part_sum is parts[0], stop=part_sum is parts[-1], skip_group_check=True)
                    mm.then_inc(sum_done, 1)
                else:
                    te.matmul(PS[:, NORM_BANK, 0:width], ones[:, :], ssq[:, 0:width], start=True, stop=True).then_inc(sum_done, 1)

            def spread(n):
                te.wait_ge(diag_done, n + 1)
                te.matmul(PS[:, NORM_BANK, :], ones[:, :], nt_a[:, :], start=True, stop=True).then_inc(spread_done, 1)

            def o_part(u_o, i, ks):
                te.wait_ge(w_lo_done, u_o + i + 1)
                te.wait_ge(exp_done, n_core * HEADS + 3 + i // 2)
                for k in ks:
                    te.wait_ge(o_lo_done, n_core * HEADS + k // 2 + 1)
                    s = slice(k * P, (k + 1) * P)
                    mm = three(PS[:, i, :], w_hi[:, i, s], w_lo[:, i, s], m_hi[:, k, :], m_lo[:, k, :], k == 0, k == KD - 1)
                if ks[-1] == KD - 1:
                    mm.then_inc(unit_done, 1)

            n_core = 0
            n_mem = 0
            for i_ph, (kind, layer, u0, t0, c0, part) in enumerate(phases):
                n = norm_of(i_ph)
                heads = n_core * HEADS
                if kind in ("up", "conv_cv"):
                    def body(g):
                        first = isinstance(g, int) and g == 0 and (kind != "up" or part[0] == 0)
                        for i in range(4):
                            bank_free(t0 + 4 * g + i)
                            ready = (lambda k: te.wait_ge(h_lo_done, h_base[n] + k + 1)) if first and i == 0 else None
                            unit(u0 + 4 * g + i, i, i, range(KD), h_hi, h_lo, True, True, ready)
                            if first and i == (n == 0):
                                sums("x", n, SEQ)
                            if first and i == (n == 0) + 1:
                                spread(n)
                    groups(te, (part[1] - part[0] if kind == "up" else KD) // 2, body,
                           peel_first=(kind != "up" or part[0] == 0))
                elif kind == "down":
                    if phases[i_ph + 1:] and phases[i_ph + 1][0] == "s5":
                        s5_turn(te, 0)
                        s5_lags(te, 0)
                    te.wait_ge(c_lo_done, c0 - 1)

                    def body(g):
                        for j in range(4):
                            bank_free(t0 + 4 * g + j)
                            last = (lambda k: te.wait_ge(c_lo_done, c0) if k == part[1] - part[0] - 1 else None) if j == 0 else None
                            if part == (0, KF):
                                for c, (a, b) in enumerate(CUTS):
                                    i = 3 * j + c
                                    unit(u0 + 12 * g + i, i % SLOTS, j, range(a, b), f_hi, f_lo, c == 0, c == 2, last)
                            else:
                                unit(u0 + 4 * g + j, j, j, range(part[1] - part[0]), m_hi, m_lo, True, True, last)
                    groups(te, 2, body)
                elif kind == "conv_b":
                    def body(g):
                        for i in range(4):
                            bank_free(t0 + 4 * g + i)
                            unit(u0 + 4 * g + i, i, i, range(KD), h_hi, h_lo, True, True)
                    groups(te, 2, body)
                elif kind == "conv_o":
                    sums("mem", layer, MEM)

                    def body(g):
                        for i in range(4):
                            bank_free(t0 + 4 * g + i)
                            ready = (lambda k: te.wait_ge(c_lo_done, c0 - KD + k + 1)) if isinstance(g, int) and g + i == 0 else None
                            unit(u0 + 4 * g + i, i, i, range(KD), m_hi, m_lo, True, True, ready)
                    groups(te, 2, body, peel_first=True)
                elif kind == "o":
                    def body(g):
                        for i in range(4):
                            if isinstance(g, int) and g == 0:
                                o_part(u0, i, range((6, 6, 4, 0)[i], KD))
                            else:
                                bank_free(t0 + 4 * g + i)
                                unit(u0 + 4 * g + i, i, i, range(KD), m_hi, m_lo, True, True)
                    groups(te, 2, body, peel_first=True)
                    n_core += 1
                elif kind == "glu":
                    def body(g):
                        if isinstance(g, int) and g:
                            sums("mem", layer, MEM)
                        for i in range(4):
                            bank_free(t0 + 4 * g + i)
                            ready = (lambda k: te.wait_ge(c_lo_done, c0 - KD + k + 1)) if isinstance(g, int) and g + i == 0 else None
                            unit(u0 + 4 * g + i, i, i, range(KD), m_hi, m_lo, True, True, ready)
                    groups(te, 4, body, peel_first=True, peel_last=True)
                elif kind == "k":
                    te.wait_ge(n_lo_done, (n_mem + 1) * (KD + 1))
                    n_mem += 1

                    def body(g):
                        for i in range(4):
                            bank_free(t0 + 4 * g + i)
                            unit(u0 + 4 * g + i, i, i, range(KD), n_hi, n_lo, True, True, width=MEM)
                            if isinstance(g, int) and g == 0 and i == 1:
                                sums("x", n, SEQ)
                            if isinstance(g, int) and g == 0 and i == 3:
                                spread(n)
                    groups(te, 2, body, peel_first=True)
                elif kind == "q":
                    def body(g):
                        for i in range(4):
                            bank_free(t0 + 4 * g + i)
                            unit(u0 + 4 * g + i, i, i, range(KD), h_hi, h_lo, True, True)
                    te.wait_ge(h_lo_done, h_base[n] + KD)
                    groups(te, 2, body)
                elif kind == "core":
                    def v(g):
                        if g == 0:
                            te.wait_ge(c_lo_done, c0 - KD + 1)
                        for i in range(4):
                            te.wait_ge(w_lo_done, u0 + 4 * g + i + 1)
                            for kk in range(2):
                                k = 2 * i + kk
                                s = slice(kk * 512, (kk + 1) * 512)
                                for mc in range(2):
                                    ms = slice(mc * P, (mc + 1) * P)
                                    mm = three(PS[:, 4 + 2 * g + mc, :], n_hi[:, k, ms], n_lo[:, k, ms], w_hi[:, i, s], w_lo[:, i, s],
                                               k == 0, k == KD - 1)
                            mm.then_inc(unit_done, 1)

                    def scores(h):
                        if h >= 2:
                            te.wait_ge(exp_done, heads + h - 1)
                        for t in range(4):
                            out_ = PS[:, 2 * (h % 2) + t // 2, (t % 2) * MEM:(t % 2 + 1) * MEM]
                            ts_ = slice(t * P, (t + 1) * P)
                            for dc in range(2):
                                k = 2 * h + dc
                                mm = three(out_, m_hi[:, k, ts_], m_lo[:, k, ts_], k_hi[:, k, :], k_lo[:, k, :], dc == 0, dc == 1)
                        mm.then_inc(score_done, 1)

                    def turn(h):
                        te.wait_ge(prob_done, heads + h + 1)
                        if h:
                            te.wait_ge(pt_lo_done, heads + h)
                        else:
                            te.wait_ge(tile_done, t0 + 2)
                        for mc in range(2):
                            for t in range(4):
                                mm = te.transpose(PS[:, 4 + mc, t * P:(t + 1) * P], prob[:, h % 2, t, mc * P:(mc + 1) * P], ident[:, :])
                        mm.then_inc(pt_done, 1)

                    def values(h):
                        te.wait_ge(pt_lo_done, heads + h + 1)
                        if h:
                            te.wait_ge(o_lo_done, heads + h)
                        else:
                            te.wait_ge(tile_done, t0 + 4)
                        for dc in range(2):
                            s = slice(h * HD + dc * P, h * HD + (dc + 1) * P)
                            for mc in range(2):
                                mm = three(PS[:, 6 + dc, :], v_hi[:, mc, s], v_lo[:, mc, s], pt_hi[:, mc, :], pt_lo[:, mc, :],
                                           mc == 0, mc == 1)
                        mm.then_inc(pv_done, 1)

                    v(0)
                    te.wait_ge(c_lo_done, c0)
                    te.wait_ge(tile_done, t0)
                    scores(0)
                    scores(1)
                    v(1)
                    turn(0)
                    scores(2)
                    values(0)
                    turn(1)
                    scores(3)
                    values(1)
                    turn(2)
                    o_part(u0 + 8, 0, range(0, 2))
                    o_part(u0 + 8, 1, range(0, 2))
                    values(2)
                    turn(3)
                    o_part(u0 + 8, 0, range(2, 4))
                    o_part(u0 + 8, 1, range(2, 4))
                    values(3)
                    o_part(u0 + 8, 0, range(4, 6))
                    o_part(u0 + 8, 1, range(4, 6))
                    o_part(u0 + 8, 2, range(0, 4))
                elif kind == "s5":
                    te.wait_ge(s5_et, 4)
                    sums("x", n, SEQ)
                    s5_turn(te, 1, range(0, 2))
                    spread(n)
                    s5_turn(te, 1, range(2, 4))
                    te.wait_ge(tile_done, t0)
                    s5_inputs(te, 0)
                    s5_within(te, 0)
                    te.wait_ge(s5_xfree, 1)
                    s5_inputs(te, 1)
                    s5_turn(te, 2)
                    for r in range(1, 4):
                        if r == 2:
                            s5_turn(te, 3)
                        s5_lags(te, r)
                        s5_outputs(te, r - 1)
                        s5_within(te, r)
                        if r < 3:
                            te.wait_ge(s5_xfree, r + 1)
                            s5_inputs(te, r + 1)
                    s5_outputs(te, 3)
            sums("x", len(RESID), SEQ)
            spread(len(RESID))



def kernel(x, mem, norm_g, final_g, ffn1_up, ffn1_down, ffn2_up, ffn2_down, conv_w_in, conv_w, conv_w_out,
           ssm_a_re, ssm_a_im, ssm_log_dt, ssm_b_re, ssm_b_im, ssm_c_re, ssm_c_im, ssm_d, ssm_w_glu,
           xa_w_q, xa_w_kv, xa_w_o):
    import numpy as np
    import concourse.bacc as bacc
    from concourse.bass_utils import run_bass_kernel_spmd

    arr = {k: np.asarray(v) for k, v in locals().items() if k not in ("np", "bacc", "run_bass_kernel_spmd")}

    def chunks(a):
        a = np.asarray(a)
        return np.ascontiguousarray(a.reshape(a.shape[0], -1, P).transpose(2, 1, 0))

    def units(w):
        k, m = w.shape
        return w.reshape(k // P, P, m // P, P).transpose(2, 1, 0, 3).reshape(m // P, P, k)

    def paired(a, b):
        return np.stack([units(a), units(b)], 1).reshape(-1, P, D)

    def moving(w):
        return w.reshape(4, 2, P, 2, 512).transpose(3, 0, 2, 1, 4).reshape(8, P, D)

    stream, down = [], []
    for l in range(DEPTH):
        up1, up2 = arr["ffn1_up"][l], arr["ffn2_up"][l]
        stream.append(paired(up1[:, :FF], up1[:, FF:]))
        down.append(units(arr["ffn1_down"][l]))
        if l % 2 == 0:
            w = arr["conv_w_in"][l // 2]
            stream += [paired(w[:, :D], w[:, 2 * D:]), units(w[:, D:2 * D]), units(arr["conv_w_out"][l // 2])]
        else:
            w = arr["ssm_w_glu"][l // 2]
            stream.append(paired(w[:, :D], w[:, D:]))
        kv = arr["xa_w_kv"][l]
        stream += [units(kv[:, :D]), units(arr["xa_w_q"][l]), moving(kv[:, D:]), units(arr["xa_w_o"][l])]
        stream.append(paired(up2[:, :FF], up2[:, FF:]))
        down.append(units(arr["ffn2_down"][l]))

    def col(v):
        return v.reshape(-1, KD, P).transpose(2, 0, 1).reshape(P, -1)

    cols = np.concatenate([col(arr["norm_g"]), col(arr["final_g"]), col(arr["conv_w"][0]), col(arr["ssm_d"])], 1)

    def states(v):
        return v.reshape(NT, P).T

    s5p = np.stack([states(arr["ssm_a_re"][0]), states(arr["ssm_a_im"][0]),
                    states(np.broadcast_to(arr["ssm_log_dt"][0][:, None], (64, 64)))], 1)

    def blocks(v):
        v = v.reshape(NT, 2, 64, 16)
        b = np.zeros((2, 64, NT, 2, 16), np.float32)
        for g in range(2):
            b[g, :, :, g, :] = v[:, g].transpose(1, 0, 2)
        return b.reshape(P, NT, 32)

    bc = np.stack([blocks(arr["ssm_b_re"][0]), blocks(arr["ssm_b_im"][0]),
                   blocks(arr["ssm_c_re"][0].transpose(0, 2, 1)), blocks(arr["ssm_c_im"][0].transpose(0, 2, 1))], 1)
    bc = bc.reshape(P, 4, 4, QT * 32).transpose(2, 0, 1, 3)

    ins = {"x_in": chunks(arr["x"][0]), "mem_in": chunks(arr["mem"][0]), "cols_in": cols,
           "w8": np.concatenate(stream), "wd": np.concatenate(down), "s5p": s5p, "s5bc": bc}
    ins = {k: np.ascontiguousarray(v) for k, v in ins.items()}
    nc = bacc.Bacc("TRN2", target_bir_lowering=False, num_devices=1)
    aps = [nc.dram_tensor(k, v.shape, F32, kind="ExternalInput").ap() for k, v in ins.items()]
    out = nc.dram_tensor("out", (P, KD, SEQ), F32, kind="ExternalOutput").ap()
    scratch = nc.dram_tensor("scratch", (4, P, 26 * QT * 32), F32, kind="Internal").ap()
    build(nc, *aps, scratch, out)
    r = run_bass_kernel_spmd(nc, [ins], core_ids=[0])
    return r.results[0]["out"].transpose(2, 1, 0).reshape(1, SEQ, D)
```
